# Optimizing a Trainium2 kernel written in Bass

```python
import jax, jax.numpy as jnp
from jax import lax
import numpy as np

D_MODEL = 1024
BATCH = 1
SEQ = 256
DEPTH = 1

HEAD_DIM = 64
N_HEADS_MOBA = 8
N_HEADS_SB = 8
D_MOBA = N_HEADS_MOBA * HEAD_DIM
D_SB = N_HEADS_SB * HEAD_DIM
MOBA_BLOCK = 256
MOBA_TOP_K = 3
Q_CHUNK = 128
ROPE_THETA = 500000.0
ROPE_DIM = HEAD_DIM // 4
D_FF = 2816
FFN_RES = 0.5
EPS = 1e-6
D_IN = 3 * D_MOBA + 3 * D_SB + 2 * D_MODEL
NEG = -1e30


def rms_norm(x, g):
    x32 = x.astype(jnp.float32)
    y = x32 * lax.rsqrt(jnp.mean(x32 * x32, axis=-1, keepdims=True) + EPS)
    return y.astype(x.dtype) * g

def swiglu(x, w_gate, w_up, w_down):
    return (jax.nn.silu(x @ w_gate) * (x @ w_up)) @ w_down

def partial_rotary(x, positions):
    half = ROPE_DIM // 2
    inv_freq = ROPE_THETA ** (-jnp.arange(half, dtype=jnp.float32) * 2.0 / ROPE_DIM)
    ang = positions.astype(jnp.float32)[:, None, :, None] * inv_freq
    cos = jnp.cos(ang).astype(x.dtype)
    sin = jnp.sin(ang).astype(x.dtype)
    x1, x2, rest = x[..., :half], x[..., half:ROPE_DIM], x[..., ROPE_DIM:]
    return jnp.concatenate([x1 * cos - x2 * sin, x2 * cos + x1 * sin, rest], axis=-1)

def split_heads(x, n):
    b, t, _ = x.shape
    return x.reshape(b, t, n, HEAD_DIM).transpose(0, 2, 1, 3)

def merge_heads(x):
    b, h, t, d = x.shape
    return x.transpose(0, 2, 1, 3).reshape(b, t, h * d)

def moba_attention(q, k, v):
    B, H, T, hd = q.shape
    nb = -(-T // MOBA_BLOCK)
    pad = nb * MOBA_BLOCK - T
    k_pad = jnp.pad(k, ((0, 0), (0, 0), (0, pad), (0, 0)))
    v_pad = jnp.pad(v, ((0, 0), (0, 0), (0, pad), (0, 0)))
    kb = k_pad.reshape(B, H, nb, MOBA_BLOCK, hd)
    vb = v_pad.reshape(B, H, nb, MOBA_BLOCK, hd)
    k_mean = jnp.mean(kb.astype(jnp.float32), axis=3)
    k_sel = min(MOBA_TOP_K, nb)
    scale = hd ** -0.5
    bi = jnp.arange(B)[:, None, None, None]
    hi = jnp.arange(H)[None, :, None, None]
    offs = jnp.arange(MOBA_BLOCK)
    blk_ids = jnp.arange(nb)

    def chunk(c):
        start = c * Q_CHUNK
        qc = lax.dynamic_slice_in_dim(q, start, Q_CHUNK, axis=2)
        t = start + jnp.arange(Q_CHUNK)
        own = start // MOBA_BLOCK
        gate = jnp.einsum('bhqd,bhnd->bhqn', qc.astype(jnp.float32), k_mean)
        gate = jnp.where(blk_ids < own, gate, NEG)
        _, idx = lax.top_k(gate, k_sel)
        valid = idx < own
        ks = kb[bi, hi, idx]
        vs = vb[bi, hi, idx]
        s_sel = jnp.einsum('bhqd,bhqkld->bhqkl', qc, ks).astype(jnp.float32) * scale
        s_sel = jnp.where(valid[..., None], s_sel, NEG).reshape(B, H, Q_CHUNK, k_sel * MOBA_BLOCK)
        k_own = lax.dynamic_index_in_dim(kb, own, axis=2, keepdims=False)
        v_own = lax.dynamic_index_in_dim(vb, own, axis=2, keepdims=False)
        s_own = jnp.einsum('bhqd,bhld->bhql', qc, k_own).astype(jnp.float32) * scale
        pos_own = own * MOBA_BLOCK + offs
        s_own = jnp.where(pos_own[None, :] <= t[:, None], s_own, NEG)
        p = jax.nn.softmax(jnp.concatenate([s_sel, s_own], axis=-1), axis=-1).astype(v.dtype)
        p_sel = p[..., :k_sel * MOBA_BLOCK].reshape(B, H, Q_CHUNK, k_sel, MOBA_BLOCK)
        p_own = p[..., k_sel * MOBA_BLOCK:]
        return (jnp.einsum('bhqkl,bhqkld->bhqd', p_sel, vs)
                + jnp.einsum('bhql,bhld->bhqd', p_own, v_own))

    out = lax.map(chunk, jnp.arange(T // Q_CHUNK))
    return out.transpose(1, 2, 0, 3, 4).reshape(B, H, T, hd)

def stick_breaking_attention(q, k, v):
    B, H, T, hd = q.shape
    scale = hd ** -0.5
    s_pos = jnp.arange(T)

    def chunk(c):
        start = c * Q_CHUNK
        qc = lax.dynamic_slice_in_dim(q, start, Q_CHUNK, axis=2)
        t = start + jnp.arange(Q_CHUNK)
        z = jnp.einsum('bhqd,bhsd->bhqs', qc, k).astype(jnp.float32) * scale
        past = s_pos[None, :] < t[:, None]
        log_fail = jnp.where(past, jax.nn.log_sigmoid(-z), 0.0)
        later = lax.cumsum(log_fail, axis=3, reverse=True) - log_fail
        w = jnp.where(past, jnp.exp(jax.nn.log_sigmoid(z) + later), 0.0)
        return jnp.einsum('bhqs,bhsd->bhqd', w.astype(v.dtype), v)

    out = lax.map(chunk, jnp.arange(T // Q_CHUNK))
    return out.transpose(1, 2, 0, 3, 4).reshape(B, H, T, hd)

def hybrid_mixer(u, positions, w_in, b_gate, w_branch_moba, w_branch_sb, w_out):
    proj = u @ w_in
    cuts = [D_MOBA, 2 * D_MOBA, 3 * D_MOBA, 3 * D_MOBA + D_SB, 3 * D_MOBA + 2 * D_SB,
            3 * D_MOBA + 3 * D_SB, 3 * D_MOBA + 3 * D_SB + D_MODEL]
    q_a, k_a, v_a, q_b, k_b, v_b, g_a, g_b = jnp.split(proj, cuts, axis=-1)
    q_a = partial_rotary(split_heads(q_a, N_HEADS_MOBA), positions)
    k_a = partial_rotary(split_heads(k_a, N_HEADS_MOBA), positions)
    y_a = merge_heads(moba_attention(q_a, k_a, split_heads(v_a, N_HEADS_MOBA)))
    y_b = merge_heads(stick_breaking_attention(split_heads(q_b, N_HEADS_SB),
                                               split_heads(k_b, N_HEADS_SB),
                                               split_heads(v_b, N_HEADS_SB)))
    gates = jax.nn.sigmoid(jnp.concatenate([g_a, g_b], axis=-1) + b_gate)
    gate_a, gate_b = gates[..., :D_MODEL], gates[..., D_MODEL:]
    merged = gate_a * (y_a @ w_branch_moba) + gate_b * (y_b @ w_branch_sb)
    return merged @ w_out

def first_inputs(seed: int = 0) -> dict:
    key = jax.random.key(seed)
    ks = jax.random.split(key, 18)

    def w(k, shape, fan_in):
        return jax.random.normal(k, shape, jnp.float32) * fan_in ** -0.5

    def gain(k):
        return 1.0 + 0.05 * jax.random.normal(k, (DEPTH, D_MODEL), jnp.float32)

    return {
        "x": jax.random.normal(ks[0], (BATCH, SEQ, D_MODEL), jnp.float32),
        "positions": jnp.broadcast_to(jnp.arange(SEQ, dtype=jnp.int32), (BATCH, SEQ)),
        "ffn1_norm": gain(ks[1]),
        "ffn1_w_gate": w(ks[2], (DEPTH, D_MODEL, D_FF), D_MODEL),
        "ffn1_w_up": w(ks[3], (DEPTH, D_MODEL, D_FF), D_MODEL),
        "ffn1_w_down": w(ks[4], (DEPTH, D_FF, D_MODEL), D_FF),
        "mix_norm": gain(ks[5]),
        "w_in": w(ks[6], (DEPTH, D_MODEL, D_IN), D_MODEL),
        "b_gate": 0.02 * jax.random.normal(ks[7], (DEPTH, 2 * D_MODEL), jnp.float32),
        "w_branch_moba": w(ks[8], (DEPTH, D_MOBA, D_MODEL), D_MOBA),
        "w_branch_sb": w(ks[9], (DEPTH, D_SB, D_MODEL), D_SB),
        "w_out": w(ks[10], (DEPTH, D_MODEL, D_MODEL), D_MODEL),
        "ffn2_norm": gain(ks[11]),
        "ffn2_w_gate": w(ks[12], (DEPTH, D_MODEL, D_FF), D_MODEL),
        "ffn2_w_up": w(ks[13], (DEPTH, D_MODEL, D_FF), D_MODEL),
        "ffn2_w_down": w(ks[14], (DEPTH, D_FF, D_MODEL), D_FF),
        "final_norm": 1.0 + 0.05 * jax.random.normal(ks[15], (D_MODEL,), jnp.float32),
    }

def first_block(x, positions, ffn1_norm, ffn1_w_gate, ffn1_w_up, ffn1_w_down, mix_norm, w_in,
              b_gate, w_branch_moba, w_branch_sb, w_out, ffn2_norm, ffn2_w_gate, ffn2_w_up,
              ffn2_w_down, final_norm):
    h = x
    for l in range(DEPTH):
        h = h + FFN_RES * swiglu(rms_norm(h, ffn1_norm[l]), ffn1_w_gate[l], ffn1_w_up[l], ffn1_w_down[l])
        h = h + hybrid_mixer(rms_norm(h, mix_norm[l]), positions, w_in[l], b_gate[l],
                             w_branch_moba[l], w_branch_sb[l], w_out[l])
        h = h + FFN_RES * swiglu(rms_norm(h, ffn2_norm[l]), ffn2_w_gate[l], ffn2_w_up[l], ffn2_w_down[l])
    return rms_norm(h, final_norm)


DEPTH_2 = 2

CHUNK = 64
N_MEM = 256
A_GROUPS = 4
A_GROUP_DIM = 128
A_WIDTH = A_GROUPS * A_GROUP_DIM
A_BLOCK = 128
FOX_HEADS = 8
FOX_HEAD_DIM = 64
FOX_WIDTH = FOX_HEADS * FOX_HEAD_DIM
Q_BLOCK = 128
POOL_WINDOWS = (2, 4, 8, 16)
POOL_GROUP_DIM = 128
POOL_WIDTH = len(POOL_WINDOWS) * POOL_GROUP_DIM
CONV_WIDTH = 512
CONV_K = 3
MIX_WIDTH = 1024
EVEN_IN = 2 * A_WIDTH + 3 * FOX_WIDTH + FOX_HEADS
ODD_IN = POOL_WIDTH + 3 * CONV_WIDTH
XA_HEADS = 4
XA_HEAD_DIM = 128
XA_WIDTH = XA_HEADS * XA_HEAD_DIM
D_FF_2 = -(-(8 * D_MODEL) // (3 * 256)) * 256
N_EVEN = (DEPTH_2 + 1) // 2
N_ODD = DEPTH_2 // 2


def rms_norm_2(x, g):
    xf = x.astype(jnp.float32)
    y = xf * lax.rsqrt(jnp.mean(xf * xf, axis=-1, keepdims=True) + EPS)
    return (y * g.astype(jnp.float32)).astype(x.dtype)

def chunk_gmlp(u, v, g_v, w_s, b_s):
    B, S, _ = v.shape
    v = rms_norm_2(v.reshape(B, S, A_GROUPS, A_GROUP_DIM), g_v.reshape(A_GROUPS, A_GROUP_DIM))
    vb = v.reshape(B, S // A_BLOCK, A_BLOCK, A_GROUPS, A_GROUP_DIM)
    cpos = np.arange(A_BLOCK) // CHUNK
    mask = jnp.asarray(cpos[:, None] >= cpos[None, :]).astype(w_s.dtype)
    w = w_s * mask[None]
    s = jnp.einsum('gts,bnsgc->bntgc', w, vb) + b_s.T[None, None, :, :, None]
    return u * s.reshape(B, S, A_WIDTH)

def forgetting_attention(q, k, v, log_f):
    B, S, H, hd = q.shape
    nb = S // Q_BLOCK
    scale = 1.0 / np.sqrt(hd)
    c = jnp.cumsum(log_f.astype(jnp.float32), axis=1).transpose(0, 2, 1)
    qb = q.reshape(B, nb, Q_BLOCK, H, hd).transpose(1, 0, 2, 3, 4)
    cb = c.reshape(B, H, nb, Q_BLOCK).transpose(2, 0, 1, 3)
    kpos = jnp.arange(S)

    def block(args):
        qi, ci, i = args
        logits = jnp.einsum('bqhd,bkhd->bhqk', qi, k).astype(jnp.float32) * scale
        logits = logits + ci[..., :, None] - c[:, :, None, :]
        qpos = i * Q_BLOCK + jnp.arange(Q_BLOCK)
        allowed = kpos[None, :] <= qpos[:, None]
        logits = jnp.where(allowed[None, None], logits, -jnp.inf)
        p = jax.nn.softmax(logits, axis=-1)
        return jnp.einsum('bhqk,bkhd->bqhd', p.astype(v.dtype), v)

    out = lax.map(block, (qb, cb, jnp.arange(nb)))
    return out.transpose(1, 0, 2, 3, 4).reshape(B, S, H * hd)

def multiscale_pool(z, w_pool, s_pool):
    B, S, _ = z.shape
    zf = z.astype(jnp.float32)
    cs = jnp.cumsum(zf, axis=1)
    pos = jnp.arange(S)
    outs = []
    for g, w in enumerate(POOL_WINDOWS):
        sl = slice(g * POOL_GROUP_DIM, (g + 1) * POOL_GROUP_DIM)
        csg = cs[..., sl]
        lag = jnp.pad(csg, ((0, 0), (w, 0), (0, 0)))[:, :S]
        cnt = jnp.minimum(pos + 1, w).astype(jnp.float32)[None, :, None]
        outs.append((csg - lag) / cnt - zf[..., sl])
    p = jnp.concatenate(outs, axis=-1).astype(z.dtype)
    p = p.reshape(B, S, len(POOL_WINDOWS), POOL_GROUP_DIM)
    y = jnp.einsum('bsgc,gcd->bsgd', p, w_pool).reshape(B, S, POOL_WIDTH)
    return y * s_pool

def short_gated_conv(h, gate_b, gate_c, conv_w):
    S = h.shape[1]
    xg = gate_c * h
    xp = jnp.pad(xg, ((0, 0), (CONV_K - 1, 0), (0, 0)))
    conv = sum(conv_w[j] * xp[:, j:j + S] for j in range(CONV_K))
    return gate_b * conv

def even_mixer(h, w_in, b_f, g_v, w_s, b_s, g_qn, g_kn, w_out):
    B, S, _ = h.shape
    z = h @ w_in
    uv = jax.nn.gelu(z[..., :2 * A_WIDTH])
    u, v = uv[..., :A_WIDTH], uv[..., A_WIDTH:]
    o = 2 * A_WIDTH
    q = z[..., o:o + FOX_WIDTH].reshape(B, S, FOX_HEADS, FOX_HEAD_DIM)
    k = z[..., o + FOX_WIDTH:o + 2 * FOX_WIDTH].reshape(B, S, FOX_HEADS, FOX_HEAD_DIM)
    vv = z[..., o + 2 * FOX_WIDTH:o + 3 * FOX_WIDTH].reshape(B, S, FOX_HEADS, FOX_HEAD_DIM)
    f_logit = z[..., o + 3 * FOX_WIDTH:].astype(jnp.float32) + b_f.astype(jnp.float32)
    log_f = jax.nn.log_sigmoid(f_logit)
    q = rms_norm_2(q, g_qn)
    k = rms_norm_2(k, g_kn)
    y_a = chunk_gmlp(u, v, g_v, w_s, b_s)
    y_b = forgetting_attention(q, k, vv, log_f).astype(h.dtype)
    return jnp.concatenate([y_a, y_b], axis=-1) @ w_out

def odd_mixer(h, w_in, w_pool, s_pool, conv_w, w_out):
    z = h @ w_in
    zc = z[..., :POOL_WIDTH]
    o = POOL_WIDTH
    hd = z[..., o:o + CONV_WIDTH]
    gb = z[..., o + CONV_WIDTH:o + 2 * CONV_WIDTH]
    gc = z[..., o + 2 * CONV_WIDTH:]
    y_c = multiscale_pool(zc, w_pool, s_pool)
    y_d = short_gated_conv(hd, gb, gc, conv_w)
    return jnp.concatenate([y_c, y_d], axis=-1) @ w_out

def memory_cross_attention(h, m, w_q, w_kv, w_o, g_qn, g_kn):
    B, S, _ = h.shape
    M = m.shape[1]
    q = rms_norm_2((h @ w_q).reshape(B, S, XA_HEADS, XA_HEAD_DIM), g_qn)
    kv = m @ w_kv
    k = rms_norm_2(kv[..., :XA_WIDTH].reshape(B, M, XA_HEADS, XA_HEAD_DIM), g_kn)
    v = kv[..., XA_WIDTH:].reshape(B, M, XA_HEADS, XA_HEAD_DIM)
    logits = jnp.einsum('bshd,bmhd->bhsm', q, k).astype(jnp.float32) / np.sqrt(XA_HEAD_DIM)
    p = jax.nn.softmax(logits, axis=-1).astype(v.dtype)
    o = jnp.einsum('bhsm,bmhd->bshd', p, v).reshape(B, S, XA_WIDTH)
    return o @ w_o

def swiglu_2(h, w_gate, w_up, w_down):
    return (jax.nn.silu(h @ w_gate) * (h @ w_up)) @ w_down

def second_inputs(seed: int = 0) -> dict:
    key = jax.random.key(seed)
    ks = jax.random.split(key, 32)
    f32 = jnp.float32

    def nrm(k, shape, scale):
        return jax.random.normal(k, shape, f32) * scale

    def gain(k, shape):
        return 1.0 + 0.05 * jax.random.normal(k, shape, f32)

    L, NE, NO, D = DEPTH_2, N_EVEN, N_ODD, D_MODEL
    return {
        "x": nrm(ks[0], (BATCH, SEQ, D), 1.0),
        "mem": nrm(ks[1], (BATCH, N_MEM, D), 1.0),
        "g_mix": gain(ks[2], (L, D)),
        "g_xa": gain(ks[3], (L, D)),
        "g_mem": gain(ks[4], (L, D)),
        "xa_wq": nrm(ks[5], (L, D, XA_WIDTH), D ** -0.5),
        "xa_wkv": nrm(ks[6], (L, D, 2 * XA_WIDTH), D ** -0.5),
        "xa_wo": nrm(ks[7], (L, XA_WIDTH, D), XA_WIDTH ** -0.5),
        "xa_gq": gain(ks[8], (L, XA_HEAD_DIM)),
        "xa_gk": gain(ks[9], (L, XA_HEAD_DIM)),
        "g_ffn": gain(ks[10], (L, D)),
        "w_gate": nrm(ks[11], (L, D, D_FF_2), D ** -0.5),
        "w_up": nrm(ks[12], (L, D, D_FF_2), D ** -0.5),
        "w_down": nrm(ks[13], (L, D_FF_2, D), D_FF_2 ** -0.5),
        "e_w_in": nrm(ks[14], (NE, D, EVEN_IN), D ** -0.5),
        "e_b_f": jnp.linspace(1.0, 6.0, FOX_HEADS, dtype=f32)[None] + 0.1 * jax.random.normal(ks[15], (NE, FOX_HEADS), f32),
        "e_g_v": gain(ks[16], (NE, A_WIDTH)),
        "e_w_s": nrm(ks[17], (NE, A_GROUPS, A_BLOCK, A_BLOCK), A_BLOCK ** -0.5),
        "e_b_s": gain(ks[18], (NE, A_GROUPS, A_BLOCK)),
        "e_g_qn": gain(ks[19], (NE, FOX_HEAD_DIM)),
        "e_g_kn": gain(ks[20], (NE, FOX_HEAD_DIM)),
        "e_w_out": nrm(ks[21], (NE, MIX_WIDTH, D), MIX_WIDTH ** -0.5),
        "o_w_in": nrm(ks[22], (NO, D, ODD_IN), D ** -0.5),
        "o_w_pool": nrm(ks[23], (NO, len(POOL_WINDOWS), POOL_GROUP_DIM, POOL_GROUP_DIM), POOL_GROUP_DIM ** -0.5),
        "o_s_pool": gain(ks[24], (NO, POOL_WIDTH)),
        "o_conv_w": nrm(ks[25], (NO, CONV_K, CONV_WIDTH), CONV_K ** -0.5),
        "o_w_out": nrm(ks[26], (NO, MIX_WIDTH, D), MIX_WIDTH ** -0.5),
    }

def second_block(x, mem, g_mix, g_xa, g_mem, xa_wq, xa_wkv, xa_wo, xa_gq, xa_gk,
              g_ffn, w_gate, w_up, w_down,
              e_w_in, e_b_f, e_g_v, e_w_s, e_b_s, e_g_qn, e_g_kn, e_w_out,
              o_w_in, o_w_pool, o_s_pool, o_conv_w, o_w_out):
    for layer in range(DEPTH_2):
        i = layer // 2
        h = rms_norm_2(x, g_mix[layer])
        if layer % 2 == 0:
            y = even_mixer(h, e_w_in[i], e_b_f[i], e_g_v[i], e_w_s[i], e_b_s[i],
                           e_g_qn[i], e_g_kn[i], e_w_out[i])
        else:
            y = odd_mixer(h, o_w_in[i], o_w_pool[i], o_s_pool[i], o_conv_w[i], o_w_out[i])
        x = x + y
        m = rms_norm_2(mem, g_mem[layer])
        x = x + memory_cross_attention(rms_norm_2(x, g_xa[layer]), m, xa_wq[layer], xa_wkv[layer],
                                       xa_wo[layer], xa_gq[layer], xa_gk[layer])
        x = x + swiglu_2(rms_norm_2(x, g_ffn[layer]), w_gate[layer], w_up[layer], w_down[layer])
    return x


def setup_inputs(seed=0):
    out = dict(first_inputs(seed))
    for name, value in second_inputs(seed + 1).items():
        if name != "x":
            out[name + "_2"] = value
    return out


def reference(
    x, positions, ffn1_norm, ffn1_w_gate, ffn1_w_up, ffn1_w_down, mix_norm, w_in, b_gate,
    w_branch_moba, w_branch_sb, w_out, ffn2_norm, ffn2_w_gate, ffn2_w_up, ffn2_w_down,
    final_norm, mem_2, g_mix_2, g_xa_2, g_mem_2, xa_wq_2, xa_wkv_2, xa_wo_2, xa_gq_2, xa_gk_2,
    g_ffn_2, w_gate_2, w_up_2, w_down_2, e_w_in_2, e_b_f_2, e_g_v_2, e_w_s_2, e_b_s_2, e_g_qn_2,
    e_g_kn_2, e_w_out_2, o_w_in_2, o_w_pool_2, o_s_pool_2, o_conv_w_2, o_w_out_2,
):
    x = first_block(
        x, positions, ffn1_norm, ffn1_w_gate, ffn1_w_up, ffn1_w_down, mix_norm, w_in, b_gate,
        w_branch_moba, w_branch_sb, w_out, ffn2_norm, ffn2_w_gate, ffn2_w_up, ffn2_w_down,
        final_norm,
    )
    return second_block(
        x, mem_2, g_mix_2, g_xa_2, g_mem_2, xa_wq_2, xa_wkv_2, xa_wo_2, xa_gq_2, xa_gk_2,
        g_ffn_2, w_gate_2, w_up_2, w_down_2, e_w_in_2, e_b_f_2, e_g_v_2, e_w_s_2, e_b_s_2,
        e_g_qn_2, e_g_kn_2, e_w_out_2, o_w_in_2, o_w_pool_2, o_s_pool_2, o_conv_w_2, o_w_out_2,
    )


_drawn_inputs = setup_inputs


def setup_inputs(seed=0):
    import zlib

    import numpy as np

    out = dict(_drawn_inputs(seed))
    spreads = {}
    factors = {'b_gate': 8.0,
     'g_xa_2': 8.0,
     'g_mem_2': 5.558,
     'xa_gq_2': 8.0,
     'xa_gk_2': 8.0,
     'e_g_qn_2': 5.912,
     'e_g_kn_2': 5.207,
     'o_s_pool_2': 2.95}
    for name, (base, spread) in spreads.items():
        noise = np.random.default_rng([zlib.crc32(name.encode()), seed]).standard_normal(out[name].shape)
        drawn = base * np.exp(spread * noise) if base else spread * noise
        out[name] = __import__('jax').numpy.asarray(drawn.astype(out[name].dtype))
    for name, factor in factors.items():
        out[name] = (out[name] * factor).astype(out[name].dtype)
    return out
```

```python
from contextlib import ExitStack

import numpy as np

import concourse.bass as bass
from concourse import mybir
from concourse.alu_op_type import AluOpType as ALU

F32 = mybir.dt.float32
F32R = mybir.dt.float32r
I32 = mybir.dt.int32
ACT = mybir.ActivationFunctionType
AX = mybir.AxisListType

P = 128
T = 256
NT = T // P
D = 1024
KT = D // P
FF = 2816
FC = 256
NFC = FF // FC
NEG = -1e30
EPS = 1e-6
ROPE_HALF = 8
POOL_WINDOWS = (2, 4, 8, 16)

UNIT = 1024
NRAW = 3
NSPLIT = 6
LEAD = 4

STREAM = [("ffn0", 66), ("w_in", 40), ("branch_sb", 4), ("branch_moba", 4), ("w_out", 8),
          ("ffn1", 66), ("e_in", 20), ("mem_k0", 4), ("mem_v0", 4), ("e_out", 8),
          ("xq0", 4), ("mem_k1", 4), ("mem_v1", 4), ("xo0", 4), ("ffn2", 66),
          ("o_in", 16), ("o_out", 8), ("xq1", 4), ("xo1", 4), ("ffn3", 66)]
FIRST = {}
TOTAL = 0
for _name, _count in STREAM:
    FIRST[_name] = TOTAL
    TOTAL += _count

ROWS = [("ffn1_norm", 8), ("mix_norm", 8), ("ffn2_norm", 8), ("g_mix_2", 16), ("g_xa_2", 16),
        ("g_mem_2", 16), ("g_ffn_2", 16), ("o_s_pool_2", 4), ("o_conv_w_2", 12), ("e_b_s_2", 4),
        ("xa_gq_2", 2), ("xa_gk_2", 2), ("e_g_qn_2", 1), ("e_g_kn_2", 1)]
COL = {}
NCOL = 0
for _name, _count in ROWS:
    COL[_name] = NCOL
    NCOL += _count

W_IN_COLS = [1536, 2048, 2560, 0, 512, 1024, 3072, 3584, 4096, 4608]
W_IN_BANKS = [0, 2, 4, 0, 2, 4, 0, 2, 0, 2]
E_IN_COLS = [1024, 1536, 0, 512, 2048]
E_IN_BANKS = [0, 2, 4, 0, 2]
O_IN_COLS = [0, 512, 1536, 1024]
O_IN_BANKS = [0, 2, 0, 2]
MIX_OUT = [(0, 0), (0, 1), (1, 0), (1, 1), (0, 2), (0, 3), (1, 2), (1, 3)]


def shape_constants():
    idx = np.arange(P)
    ident = np.eye(P, dtype=np.float32)
    tri = (idx[:, None] <= idx[None, :]).astype(np.float32)
    causal = np.zeros((P, 3 * P), np.float32)
    strict = np.zeros((P, 3 * P), np.float32)
    for lo in (0, 2 * P):
        causal[:, lo:lo + P] = np.where(idx[None, :] <= idx[:, None], 0.0, NEG)
        strict[:, lo:lo + P] = np.where(idx[None, :] < idx[:, None], 0.0, NEG)
    band = np.zeros((P, len(POOL_WINDOWS), 3 * P), np.float32)
    s = np.arange(T)[:, None]
    t = np.arange(T)[None, :]
    for g, w in enumerate(POOL_WINDOWS):
        cnt = np.minimum(t + 1, w).astype(np.float32)
        full = np.where((s <= t) & (s > t - w), np.float32(1.0) / cnt, np.float32(0.0))
        full = (full - (s == t)).astype(np.float32)
        band[:, g, 0:T] = full[0:P]
        band[:, g, T:] = full[P:, P:]
    inv_freq = (np.float32(500000.0) ** (-np.arange(ROPE_HALF, dtype=np.float32) * np.float32(2.0) / np.float32(16.0)))
    return {"c_ident": ident, "c_tri": tri, "c_causal": causal, "c_strict": strict,
            "c_band": band, "c_inv_freq": inv_freq.astype(np.float32)}


def two_pi_parts():
    left, parts = 2.0 * np.pi, []
    for _ in range(4):
        step = 2.0 ** (np.floor(np.log2(left)) - 11)
        part = float(np.floor(left / step) * step)
        parts.append(part)
        left -= part
    return parts


def two_block_kernel(nc, d, out):
    ctx = ExitStack()
    with ctx:
        def sb(name, shape, dt=F32):
            return ctx.enter_context(nc.sbuf_tensor("sb_" + name, shape, dt))

        def sem(name):
            return ctx.enter_context(nc.semaphore(name))

        raw = sb("raw", [P, NRAW, UNIT])
        wh = sb("wh", [P, NSPLIT, UNIT], F32R)
        wl = sb("wl", [P, NSPLIT, UNIT], F32R)
        x = sb("x", [P, NT, D])
        aTh = sb("aTh", [P, KT, T], F32R)
        aTl = sb("aTl", [P, KT, T], F32R)
        yTh = sb("yTh", [P, KT, T], F32R)
        yTl = sb("yTl", [P, KT, T], F32R)
        hTh = sb("hTh", [P, 2, T], F32R)
        hTl = sb("hTl", [P, 2, T], F32R)
        zeros = sb("zeros", [P, 512], F32R)
        z = sb("z", [P, NT, 6, 512])
        qkT = sb("qkT", [P, 4, 4, T])
        gates = sb("gates", [P, NT, 2 * D])
        vm0 = sb("vm0", [P, NT, 512])
        shared = sb("shared", [P, 2 * NT * 8 * 66])
        scores = sb("scores", [P, 2, 384])
        probs = sb("probs", [P, 4, 512])
        probsT = sb("probsT", [P, 2, 512])
        junk = sb("junk", [P, D])
        silu = junk[:, 0:512].rearrange("p (t c) -> p t c", t=NT)
        ident = sb("ident", [P, P])
        tri = sb("tri", [P, P])
        ones = sb("ones", [P, 384])
        causal = sb("causal", [P, 384])
        strict = sb("strict", [P, 384])
        vrows = sb("vrows", [NCOL, P])
        vecs = sb("vecs", [P, NCOL])
        ws_raw = probs[:, 0, :].rearrange("p (g s) -> p g s", g=4)
        wsT = sb("wsT", [P, 4, P])
        bfB = sb("bfB", [P, 8])
        wf = sb("wf", [P, KT, 8])
        wfh = sb("wfh", [P, KT, 8], F32R)
        wfl = sb("wfl", [P, KT, 8], F32R)
        ssq = sb("ssq", [P, 24])
        msq = sb("msq", [P, 24])
        rstd = sb("rstd", [P, 24])
        hssq = sb("hssq", [P, 4, 16])
        hmsq = sb("hmsq", [P, 4, 16])
        hr = sb("hr", [P, 4, 16])
        half_neg = sb("half_neg", [P, 16])
        rmax = sb("rmax", [P, 2, 2])
        rneg = sb("rneg", [P, 2, 2])
        rsum = sb("rsum", [P, 2, 2])
        rinv = sb("rinv", [P, 2, 2])
        logf = sb("logf", [P, NT, 8])
        logt = sb("logt", [P, NT, 8])
        pos_i = sb("pos_i", [P, NT], I32)
        pos_f = sb("pos_f", [P, NT])
        invf = sb("invf", [P, ROPE_HALF])
        ang = sb("ang", [P, NT, ROPE_HALF])
        turn = sb("turn", [P, NT, ROPE_HALF])
        turn_h = sb("turn_h", [P, NT, ROPE_HALF], F32R)
        turn_l = sb("turn_l", [P, NT, ROPE_HALF])
        turn_p = sb("turn_p", [P, NT, ROPE_HALF])
        sin_t = sb("sin_t", [P, NT, ROPE_HALF])
        cos_t = sb("cos_t", [P, NT, ROPE_HALF])

        zf = z[:, :, :, :].rearrange("p t m c -> p (t m c)")
        gf = gates[:, :, :].rearrange("p t c -> p (t c)")
        final_gain = zf[:, 0:D]
        mem_x = gf[:, 0:NT * D].rearrange("p (t c) -> p t c", t=NT)
        memT = gf[:, NT * D:].rearrange("p (k t) -> p k t", k=KT)
        band = gf[:, 0:4 * 384].rearrange("p (g t) -> p g t", g=4)
        wpool = gf[:, 4 * 384:4 * 384 + 512].rearrange("p (g d) -> p g d", g=4)
        gvB = z[:, 1, 5, :]
        hid = scores[:, :, 0:FC]
        soft = shared[:, 0:768].rearrange("p (s c) -> p s c", s=2)
        csum = shared[:, 768:1152]
        sp_sum = shared[:, 1152:1536]
        rope = shared[:, 1536:2048].rearrange("p (j h c) -> p j h c", j=4, h=16)
        aug = shared[:, :].rearrange("p (m t h c) -> p m t h c", m=2, t=NT, h=8)
        kz = shared[:, 0:1024].rearrange("p (t c) -> p t c", t=NT)
        vm = [vm0[:, :, :], shared[:, 1024:2048].rearrange("p (t c) -> p t c", t=NT)]
        qkf = qkT[:, :, :, :].rearrange("p m h t -> p (m h t)")
        augT = qkf[:, :].rearrange("p (m h t) -> p m h t", m=2, h=8)
        qTx = qkT[:, 0, :, :]
        kTm = qkT[:, 1, :, :]
        poolT = qkT[:, 0, :, :]
        convT = qkT[:, 1, :, :]
        xgT = qkf[:, 2 * 1024:2 * 1024 + 4 * 258].rearrange("p (b t) -> p b t", b=4)

        bank = [ctx.enter_context(nc.psum_tensor(f"bank{i}", [P, 512], F32)) for i in range(8)]

        def kview(ap):
            return ap.rearrange("(k p) n -> p k n", p=P)

        ffn_w = [tuple(kview(d[n][l]) for n in names) for names, l in (
            (("ffn1_w_gate", "ffn1_w_up", "ffn1_w_down"), 0),
            (("ffn2_w_gate", "ffn2_w_up", "ffn2_w_down"), 0),
            (("w_gate_2", "w_up_2", "w_down_2"), 0),
            (("w_gate_2", "w_up_2", "w_down_2"), 1))]
        ffn_gain = [COL["ffn1_norm"], COL["ffn2_norm"], COL["g_ffn_2"], COL["g_ffn_2"] + 8]
        ffn_alpha = [0.5, 0.5, 1.0, 1.0]
        FFN_NORM = [0, 2, 5, 8]
        FFN_FILL = [0, 2, 7, 10]
        MEM_STAT = [9, 10]
        FINAL_STAT = 11

        loaded = [sem(f"loaded{i}") for i in range(NRAW)]
        high_done = sem("high_done")
        low_done = sem("low_done")
        units_used = sem("units_used")
        x_loaded = [sem(f"x_loaded{i}") for i in range(2)]
        x_ready = sem("x_ready")
        x_pre = sem("x_pre")
        xt_psum = sem("xt_psum")
        a_high = sem("a_high")
        a_low = sem("a_low")
        ssq_done = sem("ssq_done")
        rstd_ready = sem("rstd_ready")
        silu_done = sem("silu_done")
        h_ready = sem("h_ready")
        ht_psum = sem("ht_psum")
        ht_high = sem("ht_high")
        ht_low = sem("ht_low")
        acc_half = sem("acc_half")
        consts_in = sem("consts_in")
        rows_in = sem("rows_in")
        rows_set = sem("rows_set")
        vecs_psum = sem("vecs_psum")
        vecs_ready = sem("vecs_ready")
        const_set = sem("const_set")
        pos_in = sem("pos_in")
        ang_ready = sem("ang_ready")
        cos_arg = sem("cos_arg")
        rope_tab = sem("rope_tab")
        rope_done = sem("rope_done")
        bias_in = sem("bias_in")
        small_in = sem("small_in")
        ws_in = sem("ws_in")
        ws_psum = sem("ws_psum")
        ws_copied = sem("ws_copied")
        ws_ready = sem("ws_ready")
        gv_in = sem("gv_in")
        ident_in = sem("ident_in")
        wf_high = sem("wf_high")
        wf_low = sem("wf_low")
        pool_chain = sem("pool_chain")
        act_chain = sem("act_chain")
        dve_chain = sem("dve_chain")
        mix_evac_a = sem("mix_evac_a")
        mix_evac_d = sem("mix_evac_d")
        gate_evac = sem("gate_evac")
        sig_done = sem("sig_done")
        mg_ready = sem("mg_ready")
        mgt_psum = sem("mgt_psum")
        mgt_high = sem("mgt_high")
        mgt_low = sem("mgt_low")
        even_evac_a = sem("even_evac_a")
        even_evac_d = sem("even_evac_d")
        sq_done = sem("sq_done")
        hssq_done = sem("hssq_done")
        hr_ready = sem("hr_ready")
        heads_normed = sem("heads_normed")
        f_psum = sem("f_psum")
        f_pre = sem("f_pre")
        f_log = sem("f_log")
        f_ready = sem("f_ready")
        cum_psum = sem("cum_psum")
        aug_ready = sem("aug_ready")
        vn_ready = sem("vn_ready")
        sgu_psum = sem("sgu_psum")
        ya_ready = sem("ya_ready")
        ya_psum = sem("ya_psum")
        ya_high = sem("ya_high")
        ya_low = sem("ya_low")
        fin_in = sem("fin_in")
        mem_in = sem("mem_in")
        mt_psum = sem("mt_psum")
        mt_evac = [sem("mt_evac_a"), sem("mt_evac_d")]
        memk_evac_a = sem("memk_evac_a")
        memk_evac_d = sem("memk_evac_d")
        memv_evac_a = sem("memv_evac_a")
        memv_evac_d = sem("memv_evac_d")
        band_in = sem("band_in")
        odd_evac_a = sem("odd_evac_a")
        odd_evac_d = sem("odd_evac_d")
        pool_psum = sem("pool_psum")
        pool_evac = [sem("pool_evac_a"), sem("pool_evac_d")]
        yc_psum = sem("yc_psum")
        yc_high = sem("yc_high")
        yc_low = sem("yc_low")
        xg_ready = sem("xg_ready")
        xgt_psum = sem("xgt_psum")
        xgt_evac = [sem("xgt_evac_a"), sem("xgt_evac_d")]
        gbt_psum = sem("gbt_psum")
        yd_ready = sem("yd_ready")
        yd_high = sem("yd_high")
        yd_low = sem("yd_low")
        stored = sem("stored")

        class HeadSems:

            def __init__(self, tag, stick=False):
                self.qt_psum = sem(tag + "_qt_psum")
                self.qt_evac_a = sem(tag + "_qt_evac_a")
                self.qt_evac_d = sem(tag + "_qt_evac_d")
                self.s_psum = sem(tag + "_s_psum")
                self.s_read = sem(tag + "_s_read")
                self.sm_exp = sem(tag + "_sm_exp")
                self.sm_probs = sem(tag + "_sm_probs")
                self.pt_psum = sem(tag + "_pt_psum")
                self.pt_evac = sem(tag + "_pt_evac")
                self.pv_psum = sem(tag + "_pv_psum")
                self.y_high = sem(tag + "_y_high")
                self.y_low = sem(tag + "_y_low")
                if stick:
                    self.soft_done = sem(tag + "_soft_done")
                    self.arg_done = sem(tag + "_arg_done")
                    self.sb_probs = sem(tag + "_sb_probs")

        mix_at, fox_at = HeadSems("mix", stick=True), HeadSems("fox")
        xa_at = [HeadSems("xa0"), HeadSems("xa1")]
        MIX_HEADS = [("sb", h) for h in range(8)] + [("moba", h) for h in range(8)]
        FOX_HEADS = [("fox", h) for h in range(8)]
        A_LAG = 3

        def head_cols(h):
            return slice(64 * h, 64 * h + 64)

        block = ctx.enter_context(nc.Block())

        @block.sync
        def _(sp):
            def free_raw(u, c=0):
                if u >= NRAW:
                    sp.wait_ge(low_done, u - NRAW + 1 + 6 * c)

            def load_square(u, w, k0, n0):
                free_raw(u)
                for j in range(2):
                    sp.dma_start(raw[:, u % NRAW, 512 * j:512 * j + 512],
                                 w[:, k0 + j, n0:n0 + 512]).then_inc(loaded[u % NRAW], 16)

            def load_chunk(u, w, n0, kts=KT):
                for i in range(kts // 2):
                    load_square(u + i, w, 2 * i, n0)

            def load_gate_up(u, f, i, chunk, c=0):
                free_raw(u, c)
                dst = raw[:, u % NRAW, :].rearrange("p (k g n) -> p g k n", k=2, g=2)
                for g in range(2):
                    sp.dma_start(dst[:, g], ffn_w[f][g][:, 2 * i:2 * i + 2, bass.ds(FC * chunk, FC)])\
                      .then_inc(loaded[u % NRAW], 16)

            def load_down(u, f, k, c=0):
                free_raw(u, c)
                for j in range(2):
                    sp.dma_start(raw[:, u % NRAW, 512 * j:512 * j + 512],
                                 ffn_w[f][2][:, bass.ds(k, 1), 512 * j:512 * j + 512])\
                      .then_inc(loaded[u % NRAW], 16)

            def load_ffn(f):
                u = FIRST[f"ffn{f}"]
                for i in range(4):
                    load_gate_up(u + i, f, i, 0)
                with sp.Fori(0, NFC - 1, 1) as c:
                    for i in range(4):
                        load_gate_up(u + 4 + i, f, i, c + 1, c)
                    for k in range(2):
                        load_down(u + 8 + k, f, 2 * c + k, c)
                for k in range(2):
                    load_down(u + 64 + k, f, 2 * (NFC - 1) + k)

            load_ffn(0)
            w_in, w_sb, w_mo = kview(d["w_in"][0]), kview(d["w_branch_sb"][0]), kview(d["w_branch_moba"][0])
            w_o = kview(d["w_out"][0])
            for m, n0 in enumerate(W_IN_COLS):
                load_chunk(FIRST["w_in"] + 4 * m, w_in, n0)
            for n in range(2):
                load_chunk(FIRST["branch_sb"] + 2 * n, w_sb, 512 * n, 4)
            for n in range(2):
                load_chunk(FIRST["branch_moba"] + 2 * n, w_mo, 512 * n, 4)
            for n in range(2):
                load_chunk(FIRST["w_out"] + 4 * n, w_o, 512 * n)
            load_ffn(1)
            e_in, e_out = kview(d["e_w_in_2"][0]), kview(d["e_w_out_2"][0])
            wkv = [kview(d["xa_wkv_2"][l]) for l in range(2)]
            wq = [kview(d["xa_wq_2"][l]) for l in range(2)]
            wo = [kview(d["xa_wo_2"][l]) for l in range(2)]
            for m, n0 in enumerate(E_IN_COLS):
                load_chunk(FIRST["e_in"] + 4 * m, e_in, n0)
            load_chunk(FIRST["mem_k0"], wkv[0], 0)
            load_chunk(FIRST["mem_v0"], wkv[0], 512)
            for i, (n, g) in enumerate(MIX_OUT):
                load_square(FIRST["e_out"] + i, e_out, 2 * g, 512 * n)
            load_chunk(FIRST["xq0"], wq[0], 0)
            load_chunk(FIRST["mem_k1"], wkv[1], 0)
            load_chunk(FIRST["mem_v1"], wkv[1], 512)
            for n in range(2):
                load_chunk(FIRST["xo0"] + 2 * n, wo[0], 512 * n, 4)
            load_ffn(2)
            o_in, o_out = kview(d["o_w_in_2"][0]), kview(d["o_w_out_2"][0])
            for m, n0 in enumerate(O_IN_COLS):
                load_chunk(FIRST["o_in"] + 4 * m, o_in, n0)
            for i, (n, g) in enumerate(MIX_OUT):
                load_square(FIRST["o_out"] + i, o_out, 2 * g, 512 * n)
            load_chunk(FIRST["xq1"], wq[1], 0)
            for n in range(2):
                load_chunk(FIRST["xo1"] + 2 * n, wo[1], 512 * n, 4)
            load_ffn(3)
            ov = out[0].rearrange("(t p) c -> p t c", p=P)
            for n in range(2):
                for t in range(NT):
                    sp.wait_ge(x_ready, 32 + 2 * n + t + 1)
                    sp.dma_start(ov[:, t, 512 * n:512 * n + 512], x[:, t, 512 * n:512 * n + 512])\
                      .then_inc(stored, 16)
            sp.wait_ge(stored, 64)

        @block.gpsimd
        def _(pool):
            links = [0]

            def link(ins):
                links[0] += 1
                ins.then_inc(pool_chain, 1)
                pool.wait_ge(pool_chain, links[0])

            pool.memset(vrows[:], 1.0).then_inc(rows_set, 1)
            pool.dma_start(pos_i[:], d["positions"].rearrange("b (t p) -> p (b t)", p=P),
                           allow_slow_non_contiguous=True).then_inc(pos_in, 16)
            fr = d["c_inv_freq"]
            pool.dma_start(invf[:], bass.AP(fr.tensor, fr.offset, [[0, P], [1, ROPE_HALF]])).then_inc(pos_in, 16)
            pool.memset(zeros[:].bitcast(F32), 0.0).then_inc(const_set, 1)
            pool.memset(ones[:], 1.0).then_inc(const_set, 1)
            pool.memset(half_neg[:], -0.5).then_inc(const_set, 1)
            pool.wait_ge(const_set, 3)
            bg = d["b_gate"]
            for t in range(NT):
                pool.dma_start(gates[:, t, :], bass.AP(bg.tensor, bg.offset, [[0, P], [1, 2 * D]])).then_inc(bias_in, 16)
            bf = d["e_b_f_2"]
            pool.dma_start(bfB[:], bass.AP(bf.tensor, bf.offset, [[0, P], [1, 8]])).then_inc(small_in, 16)
            pool.dma_start(wf[:], kview(d["e_w_in_2"][0])[:, :, 2560:2568]).then_inc(small_in, 16)

            def token_rstd(stat, n):
                pool.wait_ge(ssq_done, 2 * (n + 1))
                c = slice(2 * stat, 2 * stat + 2)
                link(pool.tensor_scalar(msq[:, c], ssq[:, c], 1.0 / D, EPS, ALU.mult, ALU.add))
                pool.tensor_tensor(rstd[:, c], msq[:, c], half_neg[:, 0:2], ALU.pow).then_inc(rstd_ready, 1)

            def head_rstd(n, slot, count, width):
                pool.wait_ge(hssq_done, n + 1)
                link(pool.tensor_scalar(hmsq[:, slot, 0:count], hssq[:, slot, 0:count], 1.0 / width, EPS, ALU.mult, ALU.add))
                pool.tensor_tensor(hr[:, slot, 0:count], hmsq[:, slot, 0:count], half_neg[:, 0:count], ALU.pow)\
                    .then_inc(hr_ready, 1)

            token_rstd(0, 0)

            pool.wait_ge(pos_in, 32)
            link(pool.tensor_copy(pos_f[:], pos_i[:]))
            for t in range(NT):
                ins = pool.tensor_scalar(ang[:, t, :], invf[:], pos_f[:, t:t + 1], None, ALU.mult)
            link(ins)
            MAGIC = 1.5 * 2.0 ** 23
            for _ in range(2):
                link(pool.tensor_scalar(turn[:], ang[:], float(1.0 / (2.0 * np.pi)), MAGIC, ALU.mult, ALU.add))
                link(pool.tensor_scalar(turn[:], turn[:], MAGIC, None, ALU.subtract))
                link(pool.tensor_copy(turn_h[:], turn[:]))
                link(pool.tensor_tensor(turn_l[:], turn[:], turn_h[:].bitcast(F32), ALU.subtract))
                for part in two_pi_parts():
                    for n_part in (turn_h[:].bitcast(F32), turn_l[:]):
                        link(pool.tensor_scalar(turn_p[:], n_part, part, None, ALU.mult))
                        link(pool.tensor_tensor(ang[:], ang[:], turn_p[:], ALU.subtract))
            pi = float(np.nextafter(np.float32(np.pi), np.float32(0)))
            pool.tensor_scalar(ang[:], ang[:], pi, -pi, ALU.min, ALU.max).then_inc(ang_ready, 1)
            pool.wait_ge(cos_arg, 1)
            pool.tensor_scalar(turn_p[:], turn_p[:], -1.0, float(np.pi / 2), ALU.mult, ALU.add).then_inc(cos_arg, 1)

            token_rstd(1, 1)
            pool.wait_ge(ws_copied, 1)
            pool.memset(wsT[64:P, :, 0:64], 0.0).then_inc(ws_ready, 1)
            pool.wait_ge(ws_ready, 1)
            pool.wait_ge(units_used, FIRST["w_out"] + 8)
            fn, mm, gv = d["final_norm"], d["mem_2"], d["e_g_v_2"]
            pool.dma_start(gvB, bass.AP(gv.tensor, gv.offset, [[0, P], [1, 512]])).then_inc(gv_in, 16)
            pool.dma_start(final_gain, bass.AP(fn.tensor, fn.offset, [[0, P], [1, D]])).then_inc(fin_in, 16)
            pool.dma_start(mem_x, mm[0].rearrange("(t p) c -> p t c", p=P)).then_inc(mem_in, 16)
            token_rstd(2, 2)
            token_rstd(FINAL_STAT, 3)
            token_rstd(3, 4)
            token_rstd(MEM_STAT[0], 5)
            head_rstd(0, 0, 16, 64)
            head_rstd(1, 1, 16, 64)
            head_rstd(2, 2, 8, 128)
            head_rstd(3, 3, 8, 128)
            token_rstd(4, 6)
            pool.wait_ge(mt_evac[0], 2)
            pool.wait_ge(mt_evac[1], 2)
            pool.dma_start(band, d["c_band"]).then_inc(band_in, 16)
            pool.dma_start(wpool, d["o_w_pool_2"][0].rearrange("g c d -> c g d")).then_inc(band_in, 16)
            head_rstd(4, 0, 8, 128)
            head_rstd(5, 3, 8, 128)
            token_rstd(5, 7)
            token_rstd(6, 8)
            token_rstd(7, 9)
            head_rstd(6, 0, 8, 128)
            token_rstd(8, 10)

        @block.scalar
        def _(act):
            links = [0]

            def link(ins):
                links[0] += 1
                ins.then_inc(act_chain, 1)
                act.wait_ge(act_chain, links[0])

            def copy(dst, src, scale=1.0):
                return act.activation(dst, src, ACT.Copy, scale=scale)

            def split(u, c=0):
                u = u + LEAD
                if isinstance(c, int):
                    u, c = u + 6 * c, 0
                    if u >= TOTAL:
                        return
                act.wait_ge(loaded[u % NRAW], 32 * (u // NRAW + 1) + 64 * c)
                if u >= NSPLIT:
                    act.wait_ge(units_used, u - NSPLIT + 1 + 6 * c)
                copy(wh[:, u % NSPLIT, :], raw[:, u % NRAW, :]).then_inc(high_done, 1)

            def splits(u, n):
                for i in range(n):
                    split(u + i)

            def xt_high(norm, fill, col):
                for g in range(4):
                    act.wait_ge(xt_psum, 4 * norm + g + 1)
                    for j in range(2):
                        copy(aTh[:, 2 * g + j, :], bank[6 + g % 2][:, T * j:T * j + T],
                             vecs[:, col + 2 * g + j:col + 2 * g + j + 1]).then_inc(a_high, 1)

            squares = [0]

            def token_ssq(stat, src):
                for t in range(NT):
                    if squares[0]:
                        act.wait_ge(ssq_done, squares[0])
                    squares[0] += 1
                    act.activation(junk[:], src[:, t, :], ACT.Square,
                                   accum_out=ssq[:, 2 * stat + t:2 * stat + t + 1]).then_inc(ssq_done, 1)

            def rs(stat, t):
                return rstd[:, 2 * stat + t:2 * stat + t + 1]

            def ffn(f):
                u, norm, fill = FIRST[f"ffn{f}"], FFN_NORM[f], FFN_FILL[f]

                def silu_step(c):
                    act.wait_ge(units_used, u + 4 + 6 * c)
                    for t in range(NT):
                        act.activation(silu[:, t, :], bank[t][:, 0:FC], ACT.Silu, scale=rs(norm, t))\
                           .then_inc(silu_done, 1)

                def ht_step(c):
                    act.wait_ge(ht_psum, NFC * f + c + 1)
                    copy(hTh[:, :, :], bank[6][:, :]).then_inc(ht_high, 1)

                def body(c):
                    for i in range(4):
                        split(u + 4 + i, c)
                    act.wait_ge(units_used, u + 8 + 6 * c)
                    for t in range(NT):
                        act.activation(silu[:, t, :], bank[t][:, 0:FC], ACT.Silu, scale=rs(norm, t))\
                           .then_inc(silu_done, 1)
                    for i in range(2):
                        split(u + 8 + i, c)
                    ht_step(c + 1)

                xt_high(norm, fill, ffn_gain[f])
                token_ssq(norm, x)
                splits(u, 4)
                act.wait_ge(rstd_ready, RSTD_ORDER[norm] + 1)
                silu_step(0)
                ht_step(0)
                looped = NFC - 1 if f < 3 else NFC - 2
                with act.Fori(0, looped, 1) as c:
                    body(c)
                for c in range(looped, NFC - 1):
                    body(c)
                splits(u + 64, 2)

            xv = d["x"][0].rearrange("(t p) c -> p t c", p=P)
            for n in range(2):
                act.dma_start(x[:, :, 512 * n:512 * n + 512], xv[:, :, 512 * n:512 * n + 512]).then_inc(x_loaded[n], 16)
            act.dma_start(ident[:], d["c_ident"]).then_inc(ident_in, 16)
            act.wait_ge(rows_set, 1)
            n_rows = 0
            for name, count in ROWS:
                src = d[name]
                width = 64 if name in ("e_g_qn_2", "e_g_kn_2") else P
                flat = bass.AP(src.tensor, src.offset, [[width, count], [1, width]])
                act.dma_start(vrows[COL[name]:COL[name] + count, 0:width], flat).then_inc(rows_in, 16)
            act.dma_start(tri[:], d["c_tri"]).then_inc(consts_in, 16)
            act.dma_start(causal[:], d["c_causal"]).then_inc(consts_in, 16)
            act.dma_start(strict[:], d["c_strict"]).then_inc(consts_in, 16)
            act.dma_start(ws_raw, d["e_w_s_2"][0].rearrange("g t s -> t g s")).then_inc(ws_in, 16)
            act.wait_ge(vecs_psum, 1)
            copy(vecs[:], bank[0][:, 0:NCOL]).then_inc(vecs_ready, 1)
            for u in range(LEAD):
                split(u - LEAD)
            act.wait_ge(vecs_ready, 1)

            ffn(0)

            u0, norm = FIRST["w_in"], 1
            xt_high(1, 1, COL["mix_norm"])
            token_ssq(1, x)
            act.wait_ge(ang_ready, 1)
            act.activation(turn_p[:], ang[:], ACT.Abs).then_inc(cos_arg, 1)
            act.activation(sin_t[:], ang[:], ACT.Sin).then_inc(rope_tab, 1)
            act.wait_ge(cos_arg, 2)
            act.activation(cos_t[:], turn_p[:], ACT.Sin).then_inc(rope_tab, 1)

            def qt_evac(at, k, scale):
                act.wait_ge(at.qt_psum, 2 * k + 1)
                copy(qkT[:, k, 0:2, :], bank[6][:, :], scale).then_inc(at.qt_evac_a, 1)

            act.wait_ge(rstd_ready, RSTD_ORDER[1] + 1)
            for m in range(6):
                splits(u0 + 4 * m, 4)
                if m == 0:
                    act.wait_ge(ws_psum, 1)
                    copy(wsT[:, :, :], bank[4][:, :]).then_inc(ws_copied, 1)
                act.wait_ge(units_used, u0 + 4 * m + 4)
                copy(z[:, 0, m, :], bank[W_IN_BANKS[m]][:, :], rs(1, 0)).then_inc(mix_evac_a, 1)
                if m == 2:
                    qt_evac(mix_at, 0, 0.125)
                if m == 3:
                    qt_evac(mix_at, 1, 1.0)
            qt_evac(mix_at, 2, 0.125)
            qt_evac(mix_at, 3, 1.0)

            def scores_step(at, heads, i):
                kind, _ = heads[i]
                act.wait_ge(at.s_read, i + 1)
                if kind == "sb":
                    s = soft[:, i % 2, :]
                    link(act.activation(s, scores[:, i % 2, :], ACT.Abs))
                    link(act.activation(s, s, ACT.Exp, scale=-1.0))
                    act.activation(s, s, ACT.Ln, bias=1.0).then_inc(at.soft_done, 1)
                    return
                if i >= 4:
                    act.wait_ge(at.pt_psum, i - 3)
                for t, (a, b) in enumerate(((0, P), (P, 3 * P))):
                    ins = act.activation(probs[:, i % 4, a:b], scores[:, i % 2, a:b], ACT.Exp,
                                         bias=rneg[:, i % 2, t:t + 1], accum_out=rsum[:, i % 2, t:t + 1])
                ins.then_inc(at.sm_exp, 1)

            def stick_step(at, heads, i):
                if heads[i][0] != "sb":
                    return
                act.wait_ge(at.arg_done, i + 1)
                if i >= 4:
                    act.wait_ge(at.pt_psum, i - 3)
                act.activation(probs[:, i % 4, 0:384], scores[:, i % 2, :], ACT.Exp).then_inc(at.sb_probs, 1)

            def pt_step(at, i, width):
                act.wait_ge(at.pt_psum, i + 1)
                if i >= 2:
                    act.wait_ge(at.pv_psum, i - 1)
                copy(probsT[:, i % 2, 0:width], bank[6][:, 0:width]).then_inc(at.pt_evac, 1)

            def y_step(at, i, kt0):
                if i % 2 == 0:
                    return
                j = i // 2
                act.wait_ge(at.pv_psum, i + 1)
                copy(yTh[:, kt0 + j, :], bank[7][:, T * (j % 2):T * (j % 2) + T]).then_inc(at.y_high, 1)

            def head_steps(at, heads, i, kt0):
                n = len(heads)
                if i < n:
                    scores_step(at, heads, i)
                if 1 <= i <= n:
                    stick_step(at, heads, i - 1)
                if A_LAG <= i < n + A_LAG:
                    pt_step(at, i - A_LAG, 384)
                if A_LAG + 1 <= i < n + A_LAG + 1:
                    y_step(at, i - A_LAG - 1, kt0)

            for i in range(20):
                split(u0 + 24 + i)
                head_steps(mix_at, MIX_HEADS, i, 0)
                if i == 17:
                    act.wait_ge(gate_evac, 8)
                    for a in (D, 0):
                        for t in range(NT):
                            act.activation(gates[:, t, a:a + D], gates[:, t, a:a + D], ACT.Sigmoid).then_inc(sig_done, 1)
            splits(FIRST["branch_moba"], 4)

            def merged_high(half):
                for g in (2 * half, 2 * half + 1):
                    act.wait_ge(mgt_psum, g + 1)
                    copy(yTh[:, 2 * g:2 * g + 2, :], bank[g][:, :]).then_inc(mgt_high, 1)

            merged_high(0)
            merged_high(1)
            splits(FIRST["w_out"], 8)

            ffn(1)

            act.wait_ge(x_pre, 4)
            token_ssq(FINAL_STAT, x)

            u0 = FIRST["e_in"]
            act.wait_ge(small_in, 32)
            copy(wfh[:, :, :], wf[:, :, :]).then_inc(wf_high, 1)
            xt_high(3, 3, COL["g_mix_2"])
            token_ssq(3, x)
            splits(u0, 4)
            act.wait_ge(rstd_ready, RSTD_ORDER[3] + 1)

            def evac(m, n_units, banks, stat, dst, done, func=ACT.Copy, tiles=(0,)):
                act.wait_ge(units_used, n_units)
                for t in tiles:
                    ins = act.activation(dst[:, t, :], bank[banks + t][:, :], func, scale=rs(stat, t))
                ins.then_inc(done, 1)

            def head_squares(src):
                act.activation(junk[:].rearrange("p (t c) -> p t c", t=NT), src, ACT.Square).then_inc(sq_done, 1)

            act.wait_ge(f_pre, 1)
            link(act.activation(logt[:], logf[:], ACT.Abs))
            link(act.activation(logt[:], logt[:], ACT.Exp, scale=-1.0))
            act.activation(logt[:], logt[:], ACT.Ln, bias=1.0).then_inc(f_log, 1)
            act.wait_ge(mem_in, 16)
            token_ssq(MEM_STAT[0], mem_x)
            for g in (0, 2):
                act.wait_ge(mt_psum, g + 1)
                copy(memT[:, 2 * g:2 * g + 2, :], bank[6][:, :]).then_inc(mt_evac[0], 1)
            evac(0, u0 + 4, 0, 3, z[:, :, 0, :], even_evac_a)
            splits(u0 + 4, 4)
            act.wait_ge(even_evac_a, 1)
            act.wait_ge(even_evac_d, 1)
            head_squares(z[:, :, 0, :])
            evac(1, u0 + 8, 2, 3, z[:, :, 1, :], even_evac_a)
            splits(u0 + 8, 4)
            act.wait_ge(even_evac_a, 2)
            act.wait_ge(even_evac_d, 2)
            act.wait_ge(hssq_done, 1)
            head_squares(z[:, :, 1, :])
            evac(2, u0 + 12, 4, 3, z[:, :, 2, :], even_evac_a, ACT.Gelu_apprx_tanh, (0, 1))
            splits(u0 + 12, 4)
            evac(3, u0 + 16, 0, 3, z[:, :, 3, :], even_evac_a, ACT.Gelu_apprx_tanh, (0, 1))
            act.wait_ge(hssq_done, 2)
            act.wait_ge(even_evac_a, 4)
            head_squares(z[:, :, 3, :])

            def aug_evac(m, gain):
                for g in (0, 2):
                    act.wait_ge(fox_at.qt_psum, 4 * m + g + 1)
                    copy(augT[0:66, m, 2 * g:2 * g + 2, :], bank[6][0:66, :], vecs[0:66, gain:gain + 1])\
                        .then_inc(fox_at.qt_evac_a, 1)

            aug_evac(0, COL["e_g_qn_2"])
            splits(u0 + 16, 4)
            evac(4, u0 + 20, 2, 3, z[:, :, 4, :], even_evac_a)
            aug_evac(1, COL["e_g_kn_2"])

            def mem_fill_high(fill, l):
                for k in range(KT):
                    col = COL["g_mem_2"] + 8 * l + k
                    copy(aTh[:, k, :], memT[:, k, :], vecs[:, col:col + 1]).then_inc(a_high, 1)

            act.wait_ge(mt_evac[0], 2)
            act.wait_ge(mt_evac[1], 2)
            mem_fill_high(4, 0)
            splits(FIRST["mem_k0"], 1)

            def ya_high_step():
                for g in range(2):
                    act.wait_ge(ya_psum, g + 1)
                    copy(yTh[:, 2 * g:2 * g + 2, :], bank[6 + g][:, :]).then_inc(ya_high, 1)

            ya_high_step()
            act.wait_ge(rstd_ready, RSTD_ORDER[9] + 1)
            for i in range(12):
                if i < 11:
                    split(FIRST["mem_k0"] + 1 + i)
                if i == 4:
                    evac(0, FIRST["mem_k0"] + 4, 0, MEM_STAT[0], kz, memk_evac_a)
                if i == 8:
                    evac(0, FIRST["mem_v0"] + 4, 2, MEM_STAT[0], vm[0], memv_evac_a)
                    act.wait_ge(memk_evac_a, 1)
                    act.wait_ge(memk_evac_d, 1)
                    act.wait_ge(hssq_done, 3)
                    head_squares(kz[:, :, :])
                head_steps(fox_at, FOX_HEADS, i, 4)
            splits(FIRST["e_out"] + 4, 4)

            def cross(l, fill):
                at, norm, u = xa_at[l], 4 + 3 * l, FIRST[f"xq{l}"]
                xt_high(norm, fill, COL["g_xa_2"] + 8 * l)
                token_ssq(norm, x)
                splits(u, 4)
                act.wait_ge(rstd_ready, RSTD_ORDER[norm] + 1)
                evac(0, u + 4, 0, norm, z[:, :, 0, :], even_evac_a)
                if l == 0:
                    mem_fill_high(6, 1)
                act.wait_ge(at.qt_psum, 1)
                copy(kTm[:, 0:2, :], bank[6][:, :], vecs[:, COL["xa_gk_2"] + l:COL["xa_gk_2"] + l + 1])\
                    .then_inc(at.qt_evac_a, 1)
                act.wait_ge(even_evac_a, 6 + l)
                act.wait_ge(even_evac_d, 4 + l)
                head_squares(z[:, :, 0, :])
                if l == 0:
                    splits(FIRST["mem_k1"], 4)
                act.wait_ge(at.qt_psum, 3)
                copy(qTx[:, 0:2, :], bank[6][:, :], vecs[:, COL["xa_gq_2"] + l:COL["xa_gq_2"] + l + 1])\
                    .then_inc(at.qt_evac_a, 1)
                if l == 0:
                    evac(0, FIRST["mem_k1"] + 4, 2, MEM_STAT[0], kz, memk_evac_a)
                for i in range(7):
                    if l == 0 and i < 4:
                        split(FIRST["mem_v1"] + i)
                    if i < 4:
                        act.wait_ge(at.s_read, i + 1)
                        for t in range(NT):
                            ins = act.activation(probs[:, i, T * t:T * t + T], bank[4 + i % 2][:, T * t:T * t + T],
                                                 ACT.Exp, bias=rneg[:, i % 2, t:t + 1], scale=P ** -0.5,
                                                 accum_out=rsum[:, i % 2, t:t + 1])
                        ins.then_inc(at.sm_exp, 1)
                    if 2 <= i < 6:
                        pt_step(at, i - 2, 512)
                    if 3 <= i:
                        act.wait_ge(at.pv_psum, i - 2)
                        copy(yTh[:, i - 3, :], bank[7][:, 0:T]).then_inc(at.y_high, 1)
                if l == 0:
                    evac(0, FIRST["mem_v1"] + 4, 0, MEM_STAT[0], vm[1], memv_evac_a)
                    act.wait_ge(memk_evac_a, 2)
                    act.wait_ge(memk_evac_d, 2)
                    head_squares(kz[:, :, :])
                splits(FIRST[f"xo{l}"], 4)

            cross(0, 5)
            ffn(2)

            u0 = FIRST["o_in"]
            xt_high(6, 8, COL["g_mix_2"] + 8)
            token_ssq(6, x)
            splits(u0, 4)
            act.wait_ge(rstd_ready, RSTD_ORDER[6] + 1)
            evac(0, u0 + 4, 0, 6, z[:, :, 0, :], odd_evac_a)
            splits(u0 + 4, 4)
            evac(1, u0 + 8, 2, 6, z[:, :, 1, :], odd_evac_a)
            act.wait_ge(pool_psum, 1)
            copy(poolT[:, 0:2, :], bank[4][:, :]).then_inc(pool_evac[0], 1)
            splits(u0 + 8, 4)
            evac(2, u0 + 12, 0, 6, z[:, :, 2, :], odd_evac_a)
            for g in range(4):
                act.wait_ge(yc_psum, g // 2 + 1)
                copy(yTh[:, g, :], bank[6 + g // 2][:, T * (g % 2):T * (g % 2) + T],
                     vecs[:, COL["o_s_pool_2"] + g:COL["o_s_pool_2"] + g + 1]).then_inc(yc_high, 1)
            splits(u0 + 12, 4)
            evac(3, u0 + 16, 2, 6, z[:, :, 3, :], odd_evac_a)
            act.wait_ge(xgt_psum, 1)
            copy(xgT[:, 0:2, 2:258], bank[4][:, :]).then_inc(xgt_evac[0], 1)
            splits(FIRST["o_out"], 4)
            for g in range(2):
                act.wait_ge(yd_ready, g + 1)
                copy(yTh[:, 4 + 2 * g:6 + 2 * g, :], convT[:, 2 * g:2 * g + 2, :]).then_inc(yd_high, 1)
            splits(FIRST["o_out"] + 4, 4)

            cross(1, 9)
            ffn(3)

        @block.vector
        def _(dve):
            links = [0]

            def link(ins):
                links[0] += 1
                ins.then_inc(dve_chain, 1)
                dve.wait_ge(dve_chain, links[0])

            def rs(stat, t):
                return rstd[:, 2 * stat + t:2 * stat + t + 1]

            def split(u, c=0):
                u = u + LEAD
                if isinstance(c, int):
                    u, c = u + 6 * c, 0
                    if u >= TOTAL:
                        return
                dve.wait_ge(high_done, u + 1 + 6 * c)
                dve.tensor_tensor(wl[:, u % NSPLIT, :], raw[:, u % NRAW, :],
                                  wh[:, u % NSPLIT, :].bitcast(F32), ALU.subtract).then_inc(low_done, 1)

            def splits(u, n):
                for i in range(n):
                    split(u + i)

            def xt_low(fill, col):
                for g in range(4):
                    dve.wait_ge(a_high, 8 * fill + 2 * g + 2)
                    for j in range(2):
                        k = 2 * g + j
                        dve.scalar_tensor_tensor(aTl[:, k, :], bank[6 + g % 2][:, T * j:T * j + T],
                                                 vecs[:, col + k:col + k + 1], aTh[:, k, :].bitcast(F32),
                                                 ALU.mult, ALU.subtract).then_inc(a_low, 1)

            def x_update(half, first_bank, alpha, done):
                c = slice(512 * half, 512 * half + 512)
                for t in range(NT):
                    dve.scalar_tensor_tensor(x[:, t, c], bank[first_bank + t][:, :], alpha, x[:, t, c],
                                             ALU.mult, ALU.add).then_inc(done, 1)

            def ffn(f, done):
                u, norm, fill = FIRST[f"ffn{f}"], FFN_NORM[f], FFN_FILL[f]

                def mul_step(c):
                    for t in range(NT):
                        dve.wait_ge(silu_done, 2 * NFC * f + t + 1 + 2 * c)
                        dve.scalar_tensor_tensor(hid[:, t, :], bank[t][:, FC:2 * FC], rs(norm, t), silu[:, t, :],
                                                 ALU.mult, ALU.mult).then_inc(h_ready, 1)

                def ht_step(c):
                    dve.wait_ge(ht_high, NFC * f + c + 1)
                    dve.tensor_tensor(hTl[:, :, :], bank[6][:, :], hTh[:, :, :].bitcast(F32), ALU.subtract)\
                       .then_inc(ht_low, 1)

                def body(c):
                    for i in range(4):
                        split(u + 4 + i, c)
                    mul_step(c + 1)
                    for i in range(2):
                        split(u + 8 + i, c)
                    ht_step(c + 1)

                xt_low(fill, ffn_gain[f])
                splits(u, 4)
                mul_step(0)
                ht_step(0)
                looped = NFC - 1 if f < 3 else NFC - 2
                with dve.Fori(0, looped, 1) as c:
                    body(c)
                for c in range(looped, NFC - 1):
                    body(c)
                splits(u + 64, 2)
                dve.wait_ge(acc_half, f + 1)
                x_update(0, 2, ffn_alpha[f], done)
                dve.wait_ge(units_used, u + 66)
                x_update(1, 4, ffn_alpha[f], done)

            for u in range(LEAD):
                split(u - LEAD)
            dve.wait_ge(vecs_ready, 1)
            col = COL["e_g_qn_2"]
            link(dve.tensor_scalar(vecs[0:64, col:col + 1], vecs[0:64, col:col + 1], 0.125, None, ALU.mult))

            ffn(0, x_ready)

            u0 = FIRST["w_in"]
            xt_low(1, COL["mix_norm"])
            dve.wait_ge(rstd_ready, RSTD_ORDER[1] + 1)
            dve.wait_ge(consts_in, 48)

            def evac(n_units, banks, stat, dst, done):
                dve.wait_ge(units_used, n_units)
                dve.tensor_scalar(dst[:, 1, :], bank[banks + 1][:, :], rs(stat, 1), None, ALU.mult).then_inc(done, 1)

            def qt_evac(at, k, scale):
                dve.wait_ge(at.qt_psum, 2 * k + 2)
                dve.tensor_scalar(qkT[:, k, 2:4, :], bank[7][:, :].rearrange("p (h t) -> p h t", h=2), scale, None, ALU.mult)\
                   .then_inc(at.qt_evac_d, 1)

            def rotate():
                dve.wait_ge(mix_evac_a, 5)
                dve.wait_ge(mix_evac_d, 5)
                dve.wait_ge(rope_tab, 2)
                for t in range(NT):
                    heads = z[:, t, 3:5, :].rearrange("p m (h c) -> p (m h) c", c=64)
                    x1, x2 = heads[:, :, 0:ROPE_HALF], heads[:, :, ROPE_HALF:2 * ROPE_HALF]
                    cos = cos_t[:, t:t + 1, :].broadcast_to([P, 16, ROPE_HALF])
                    sin = sin_t[:, t:t + 1, :].broadcast_to([P, 16, ROPE_HALF])
                    dve.tensor_tensor(rope[:, 0], x1, cos, ALU.mult)
                    dve.tensor_tensor(rope[:, 1], x2, sin, ALU.mult)
                    dve.tensor_tensor(rope[:, 2], x2, cos, ALU.mult)
                    link(dve.tensor_tensor(rope[:, 3], x1, sin, ALU.mult))
                    dve.tensor_tensor(x1, rope[:, 0], rope[:, 1], ALU.subtract)
                    last = dve.tensor_tensor(x2, rope[:, 2], rope[:, 3], ALU.add)
                    if t == 0:
                        link(last)
                last.then_inc(rope_done, 1)

            for m in range(6):
                splits(u0 + 4 * m, 4)
                evac(u0 + 4 * m + 4, W_IN_BANKS[m], 1, z[:, :, m, :], mix_evac_d)
                if m == 2:
                    qt_evac(mix_at, 0, 0.125)
                if m == 3:
                    qt_evac(mix_at, 1, 1.0)
                if m == 4:
                    rotate()
            qt_evac(mix_at, 2, 0.125)
            qt_evac(mix_at, 3, 1.0)

            def scores_step(at, heads, i):
                kind, _ = heads[i]
                bias = strict if kind == "sb" else causal
                dve.wait_ge(at.s_psum, i + 1)
                if i >= 2:
                    before = heads[i - 2][0]
                    if before == "sb":
                        dve.wait_ge(at.sb_probs, i - 1)
                    else:
                        n_sb = sum(k == "sb" for k, _ in heads)
                        dve.wait_ge(at.sm_exp, i - 1 - n_sb)
                s = scores[:, i % 2, :]
                ins = dve.tensor_tensor(s, bank[4 + i % 2][:, 0:384], bias[:, :], ALU.add)
                if kind == "sb":
                    ins.then_inc(at.s_read, 1)
                    return
                link(ins)
                dve.tensor_reduce(rneg[:, i % 2, 0:1], s[:, 0:P], AX.X, ALU.max, negate=True)
                dve.tensor_reduce(rneg[:, i % 2, 1:2], s[:, P:384], AX.X, ALU.max, negate=True).then_inc(at.s_read, 1)

            def weights_step(at, heads, i):
                kind, _ = heads[i]
                n_sb = sum(k == "sb" for k, _ in heads)
                if kind == "sb":
                    s, q = scores[:, i % 2, :], sp_sum
                    dve.wait_ge(at.soft_done, i + 1)
                    link(dve.scalar_tensor_tensor(q[:, :], s, 0.0, soft[:, i % 2, :], ALU.max, ALU.add))
                    for a, b in ((0, P), (P, 384)):
                        ins = dve.tensor_tensor_scan(csum[:, a:b][:, ::-1], ones[:, a:b], q[:, a:b][:, ::-1], 0.0,
                                                     ALU.mult, ALU.add)
                    link(ins)
                    dve.tensor_tensor(s, s, csum[:, :], ALU.subtract).then_inc(at.arg_done, 1)
                    return
                dve.wait_ge(at.sm_exp, i + 1 - n_sb)
                link(dve.reciprocal(rinv[:, i % 2, :], rsum[:, i % 2, :]))
                for t, (a, b) in enumerate(((0, P), (P, 384))):
                    ins = dve.tensor_scalar(probs[:, i % 4, a:b], probs[:, i % 4, a:b], rinv[:, i % 2, t:t + 1], None, ALU.mult)
                ins.then_inc(at.sm_probs, 1)

            def y_step(at, i, kt0):
                if i % 2 == 0:
                    return
                j = i // 2
                dve.wait_ge(at.y_high, j + 1)
                dve.tensor_tensor(yTl[:, kt0 + j, :], bank[7][:, T * (j % 2):T * (j % 2) + T],
                                  yTh[:, kt0 + j, :].bitcast(F32), ALU.subtract).then_inc(at.y_low, 1)

            def head_steps(at, heads, i, kt0):
                n = len(heads)
                if i < n:
                    scores_step(at, heads, i)
                if 1 <= i <= n:
                    weights_step(at, heads, i - 1)
                if A_LAG + 1 <= i < n + A_LAG + 1:
                    y_step(at, i - A_LAG - 1, kt0)

            dve.wait_ge(bias_in, 32)
            for i in range(20):
                split(u0 + 24 + i)
                head_steps(mix_at, MIX_HEADS, i, 0)
                if i % 4 == 0 and 4 <= i <= 16:
                    m = 6 + (i - 4) // 4
                    c = slice(512 * (m - 6), 512 * (m - 6) + 512)
                    dve.wait_ge(units_used, u0 + 4 * m + 4)
                    for t in range(NT):
                        dve.scalar_tensor_tensor(gates[:, t, c], bank[W_IN_BANKS[m] + t][:, :], rs(1, t), gates[:, t, c],
                                                 ALU.mult, ALU.add).then_inc(gate_evac, 1)
            splits(FIRST["branch_moba"], 2)
            for n in range(2):
                c = slice(D + 512 * n, D + 512 * n + 512)
                dve.wait_ge(units_used, FIRST["branch_sb"] + 2 * n + 2)
                dve.wait_ge(sig_done, 2)
                for t in range(NT):
                    ins = dve.tensor_tensor(gates[:, t, c], gates[:, t, c], bank[2 * n + t][:, :], ALU.mult)
                link(ins)
            splits(FIRST["branch_moba"] + 2, 2)

            def merge(n):
                a, b = slice(512 * n, 512 * n + 512), slice(D + 512 * n, D + 512 * n + 512)
                dve.wait_ge(units_used, FIRST["branch_moba"] + 2 * n + 2)
                dve.wait_ge(sig_done, 4)
                for t in range(NT):
                    ins = dve.tensor_tensor(gates[:, t, a], gates[:, t, a], bank[4 + 2 * n + t][:, :], ALU.mult)
                link(ins)
                for t in range(NT):
                    dve.tensor_tensor(gates[:, t, a], gates[:, t, a], gates[:, t, b], ALU.add).then_inc(mg_ready, 1)

            def merged_low(half):
                for g in (2 * half, 2 * half + 1):
                    dve.wait_ge(mgt_high, g + 1)
                    dve.tensor_tensor(yTl[:, 2 * g:2 * g + 2, :], bank[g][:, :], yTh[:, 2 * g:2 * g + 2, :].bitcast(F32),
                                      ALU.subtract).then_inc(mgt_low, 1)

            merge(0)
            merged_low(0)
            merge(1)
            merged_low(1)
            splits(FIRST["w_out"], 4)
            dve.wait_ge(units_used, FIRST["w_out"] + 4)
            x_update(0, 4, 1.0, x_ready)
            splits(FIRST["w_out"] + 4, 4)
            dve.wait_ge(units_used, FIRST["w_out"] + 8)
            x_update(1, 2, 1.0, x_ready)

            ffn(1, x_pre)

            dve.wait_ge(fin_in, 16)
            dve.wait_ge(rstd_ready, RSTD_ORDER[FINAL_STAT] + 1)
            for half in range(2):
                c = slice(512 * half, 512 * half + 512)
                for t in range(NT):
                    dve.scalar_tensor_tensor(x[:, t, c], x[:, t, c], rs(FINAL_STAT, t), final_gain[:, c],
                                             ALU.mult, ALU.mult).then_inc(x_ready, 1)

            u0 = FIRST["e_in"]
            dve.wait_ge(wf_high, 1)
            dve.tensor_tensor(wfl[:, :, :], wf[:, :, :], wfh[:, :, :].bitcast(F32), ALU.subtract).then_inc(wf_low, 1)
            xt_low(3, COL["g_mix_2"])
            dve.memset(aug[:, 0, :, :, 64:65], 1.0)
            dve.memset(aug[:, 1, :, :, 65:66], 1.0)
            splits(u0, 4)
            dve.wait_ge(rstd_ready, RSTD_ORDER[3] + 1)
            dve.wait_ge(f_psum, 1)
            dve.wait_ge(small_in, 32)
            for t in range(NT):
                ins = dve.scalar_tensor_tensor(logf[:, t, :], bank[4 + t][:, 0:8], rs(3, t), bfB[:, :], ALU.mult, ALU.add)
            ins.then_inc(f_pre, 1)
            dve.wait_ge(f_log, 1)
            dve.scalar_tensor_tensor(logf[:, :, :], logf[:, :, :], 0.0, logt[:, :, :], ALU.min, ALU.subtract).then_inc(f_ready, 1)
            for g in (1, 3):
                dve.wait_ge(mt_psum, g + 1)
                dve.tensor_copy(memT[:, 2 * g:2 * g + 2, :], bank[7][:, :].rearrange("p (k t) -> p k t", k=2))\
                   .then_inc(mt_evac[1], 1)
            dve.wait_ge(cum_psum, 1)
            cum = bank[5][:, 0:16].rearrange("p (t h) -> p t h", t=NT)
            dve.tensor_copy(aug[:, 0, :, :, 65], cum)
            dve.tensor_scalar(aug[:, 1, :, :, 64], cum, -1.0, None, ALU.mult).then_inc(aug_ready, 1)

            def head_sums(n, slot, heads):
                dve.wait_ge(sq_done, n + 1)
                dve.tensor_reduce(hssq[:, slot, 0:NT * heads], junk[:].rearrange("p (h c) -> p h c", h=NT * heads),
                                  AX.X, ALU.add).then_inc(hssq_done, 1)

            def head_scale(n, slot, heads, src, dst):
                dve.wait_ge(hr_ready, n + 1)
                r = hr[:, slot, 0:NT * heads].rearrange("p (t h) -> p t h", t=NT)
                w = 512 // heads
                s = src.rearrange("p t (h c) -> p t h c", h=heads)
                for t in range(NT):
                    ins = dve.tensor_tensor(dst[:, t], s[:, t], r[:, t, :].unsqueeze(2).broadcast_to([P, heads, w]), ALU.mult)
                return ins

            evac(u0 + 4, 0, 3, z[:, :, 0, :], even_evac_d)
            splits(u0 + 4, 4)
            head_sums(0, 0, 8)
            evac(u0 + 8, 2, 3, z[:, :, 1, :], even_evac_d)
            head_scale(0, 0, 8, z[:, :, 0, :], aug[:, 0, :, :, 0:64]).then_inc(heads_normed, 1)
            splits(u0 + 8, 4)
            head_sums(1, 1, 8)
            splits(u0 + 12, 4)
            head_scale(1, 1, 8, z[:, :, 1, :], aug[:, 1, :, :, 0:64]).then_inc(heads_normed, 1)
            head_sums(2, 2, 4)

            def aug_evac(m, gain):
                for g in (1, 3):
                    dve.wait_ge(fox_at.qt_psum, 4 * m + g + 1)
                    dve.tensor_scalar(augT[0:66, m, 2 * g:2 * g + 2, :],
                                      bank[7][0:66, :].rearrange("p (h t) -> p h t", h=2),
                                      vecs[0:66, gain:gain + 1], None, ALU.mult).then_inc(fox_at.qt_evac_d, 1)

            aug_evac(0, COL["e_g_qn_2"])
            v3 = z[:, :, 3, :]
            link(head_scale(2, 2, 4, v3, v3.rearrange("p t (h c) -> p t h c", h=4)))
            dve.wait_ge(gv_in, 16)
            for t in range(NT):
                ins = dve.tensor_tensor(v3[:, t, :], v3[:, t, :], gvB, ALU.mult)
            ins.then_inc(vn_ready, 1)
            splits(u0 + 16, 4)
            evac(u0 + 20, 2, 3, z[:, :, 4, :], even_evac_d)
            aug_evac(1, COL["e_g_kn_2"])
            dve.wait_ge(sgu_psum, 1)
            for t in range(NT):
                for g in range(4):
                    c = slice(P * g, P * g + P)
                    ins = dve.scalar_tensor_tensor(z[:, t, 2, c], bank[4 + t][:, c],
                                                   vecs[:, COL["e_b_s_2"] + g:COL["e_b_s_2"] + g + 1], z[:, t, 2, c],
                                                   ALU.add, ALU.mult)
                ins.then_inc(ya_ready, 1)

            def mem_fill_low(fill, l):
                for k in range(KT):
                    col = COL["g_mem_2"] + 8 * l + k
                    dve.wait_ge(a_high, 8 * fill + k + 1)
                    dve.scalar_tensor_tensor(aTl[:, k, :], memT[:, k, :], vecs[:, col:col + 1],
                                             aTh[:, k, :].bitcast(F32), ALU.mult, ALU.subtract).then_inc(a_low, 1)

            mem_fill_low(4, 0)
            splits(FIRST["mem_k0"], 1)
            for g in range(2):
                dve.wait_ge(ya_high, g + 1)
                dve.tensor_tensor(yTl[:, 2 * g:2 * g + 2, :], bank[6 + g][:, :], yTh[:, 2 * g:2 * g + 2, :].bitcast(F32),
                                  ALU.subtract).then_inc(ya_low, 1)
            dve.wait_ge(rstd_ready, RSTD_ORDER[9] + 1)
            for i in range(12):
                if i < 11:
                    split(FIRST["mem_k0"] + 1 + i)
                if i == 4:
                    evac(FIRST["mem_k0"] + 4, 0, MEM_STAT[0], kz, memk_evac_d)
                if i == 8:
                    evac(FIRST["mem_v0"] + 4, 2, MEM_STAT[0], vm[0], memv_evac_d)
                head_steps(fox_at, FOX_HEADS, i, 4)
            head_sums(3, 3, 4)
            splits(FIRST["e_out"] + 4, 4)
            head_scale(3, 3, 4, kz[:, :, :], kz[:, :, :].rearrange("p t (h c) -> p t h c", h=4)).then_inc(heads_normed, 1)
            dve.wait_ge(units_used, FIRST["e_out"] + 6)
            x_update(0, 0, 1.0, x_ready)
            dve.wait_ge(units_used, FIRST["e_out"] + 8)
            x_update(1, 2, 1.0, x_ready)

            def cross(l, fill, n_heads_normed, n_sq):
                at, norm, u = xa_at[l], 4 + 3 * l, FIRST[f"xq{l}"]
                xt_low(fill, COL["g_xa_2"] + 8 * l)
                splits(u, 4)
                dve.wait_ge(rstd_ready, RSTD_ORDER[norm] + 1)
                evac(u + 4, 0, norm, z[:, :, 0, :], even_evac_d)
                if l == 0:
                    mem_fill_low(6, 1)
                dve.wait_ge(at.qt_psum, 2)
                dve.tensor_scalar(kTm[:, 2:4, :], bank[7][:, :].rearrange("p (h t) -> p h t", h=2),
                                  vecs[:, COL["xa_gk_2"] + l:COL["xa_gk_2"] + l + 1], None, ALU.mult).then_inc(at.qt_evac_d, 1)
                head_sums(n_sq, 0, 4)
                if l == 0:
                    splits(FIRST["mem_k1"], 4)
                q = z[:, :, 0, :]
                head_scale(n_sq, 0, 4, q, q.rearrange("p t (h c) -> p t h c", h=4)).then_inc(heads_normed, 1)
                dve.wait_ge(at.qt_psum, 4)
                dve.tensor_scalar(qTx[:, 2:4, :], bank[7][:, :].rearrange("p (h t) -> p h t", h=2),
                                  vecs[:, COL["xa_gq_2"] + l:COL["xa_gq_2"] + l + 1], None, ALU.mult).then_inc(at.qt_evac_d, 1)
                if l == 0:
                    evac(FIRST["mem_k1"] + 4, 2, MEM_STAT[0], kz, memk_evac_d)
                for i in range(7):
                    if l == 0 and i < 4:
                        split(FIRST["mem_v1"] + i)
                    if i < 4:
                        dve.wait_ge(at.s_psum, i + 1)
                        link(dve.tensor_reduce(rmax[:, i % 2, :], bank[4 + i % 2][:, :].rearrange("p (t m) -> p t m", t=NT),
                                               AX.X, ALU.max))
                        dve.tensor_scalar(rneg[:, i % 2, :], rmax[:, i % 2, :], -(P ** -0.5), None, ALU.mult).then_inc(at.s_read, 1)
                    if 1 <= i < 5:
                        j = i - 1
                        dve.wait_ge(at.sm_exp, j + 1)
                        link(dve.reciprocal(rinv[:, j % 2, :], rsum[:, j % 2, :]))
                        for t in range(NT):
                            p = probs[:, j, T * t:T * t + T]
                            ins = dve.tensor_scalar(p, p, rinv[:, j % 2, t:t + 1], None, ALU.mult)
                        ins.then_inc(at.sm_probs, 1)
                    if 3 <= i:
                        dve.wait_ge(at.y_high, i - 2)
                        dve.tensor_tensor(yTl[:, i - 3, :], bank[7][:, 0:T], yTh[:, i - 3, :].bitcast(F32), ALU.subtract)\
                           .then_inc(at.y_low, 1)
                if l == 0:
                    evac(FIRST["mem_v1"] + 4, 0, MEM_STAT[0], vm[1], memv_evac_d)
                    head_sums(5, 3, 4)
                splits(FIRST[f"xo{l}"], 4)
                if l == 0:
                    head_scale(5, 3, 4, kz[:, :, :], kz[:, :, :].rearrange("p t (h c) -> p t h c", h=4)).then_inc(heads_normed, 1)
                for half in range(2):
                    dve.wait_ge(units_used, FIRST[f"xo{l}"] + 2 * half + 2)
                    x_update(half, 2 * half, 1.0, x_ready)

            cross(0, 5, 4, 4)
            ffn(2, x_ready)

            u0 = FIRST["o_in"]
            xt_low(8, COL["g_mix_2"] + 8)
            dve.memset(xgT[:, :, 0:2], 0.0)
            splits(u0, 4)
            dve.wait_ge(rstd_ready, RSTD_ORDER[6] + 1)
            evac(u0 + 4, 0, 6, z[:, :, 0, :], odd_evac_d)
            splits(u0 + 4, 4)
            evac(u0 + 8, 2, 6, z[:, :, 1, :], odd_evac_d)
            dve.wait_ge(pool_psum, 2)
            dve.tensor_copy(poolT[:, 2:4, :], bank[5][:, :].rearrange("p (g t) -> p g t", g=2)).then_inc(pool_evac[1], 1)
            splits(u0 + 8, 4)
            evac(u0 + 12, 0, 6, z[:, :, 2, :], odd_evac_d)
            dve.wait_ge(odd_evac_a, 3)
            dve.wait_ge(odd_evac_d, 3)
            dve.tensor_tensor(z[:, :, 1, :], z[:, :, 1, :], z[:, :, 2, :], ALU.mult).then_inc(xg_ready, 1)
            for g in range(4):
                dve.wait_ge(yc_high, 2 * (g // 2) + 2)
                dve.scalar_tensor_tensor(yTl[:, g, :], bank[6 + g // 2][:, T * (g % 2):T * (g % 2) + T],
                                         vecs[:, COL["o_s_pool_2"] + g:COL["o_s_pool_2"] + g + 1],
                                         yTh[:, g, :].bitcast(F32), ALU.mult, ALU.subtract).then_inc(yc_low, 1)
            splits(u0 + 12, 4)
            evac(u0 + 16, 2, 6, z[:, :, 3, :], odd_evac_d)
            dve.wait_ge(xgt_psum, 2)
            dve.tensor_copy(xgT[:, 2:4, 2:258], bank[5][:, :].rearrange("p (b t) -> p b t", b=2)).then_inc(xgt_evac[1], 1)
            dve.wait_ge(xgt_evac[0], 1)
            dve.wait_ge(xgt_evac[1], 1)

            def tap(b, j):
                return vecs[:, COL["o_conv_w_2"] + 4 * j + b:COL["o_conv_w_2"] + 4 * j + b + 1]

            for b in range(4):
                ins = dve.tensor_scalar(convT[:, b, :], xgT[:, b, 0:T], tap(b, 0), None, ALU.mult)
            link(ins)
            for j in (1, 2):
                for b in range(4):
                    ins = dve.scalar_tensor_tensor(convT[:, b, :], xgT[:, b, j:j + T], tap(b, j), convT[:, b, :], ALU.mult, ALU.add)
                link(ins)
            for g in range(2):
                dve.wait_ge(gbt_psum, g + 1)
                dve.tensor_tensor(convT[:, 2 * g:2 * g + 2, :], convT[:, 2 * g:2 * g + 2, :],
                                  bank[6 + g][:, :].rearrange("p (b t) -> p b t", b=2), ALU.mult).then_inc(yd_ready, 1)
            splits(FIRST["o_out"], 4)
            for g in range(2):
                dve.wait_ge(yd_high, g + 1)
                dve.tensor_tensor(yTl[:, 4 + 2 * g:6 + 2 * g, :], convT[:, 2 * g:2 * g + 2, :],
                                  yTh[:, 4 + 2 * g:6 + 2 * g, :].bitcast(F32), ALU.subtract).then_inc(yd_low, 1)
            splits(FIRST["o_out"] + 4, 4)
            dve.wait_ge(units_used, FIRST["o_out"] + 6)
            x_update(0, 0, 1.0, x_ready)
            dve.wait_ge(units_used, FIRST["o_out"] + 8)
            x_update(1, 2, 1.0, x_ready)

            cross(1, 9, 6, 6)
            ffn(3, x_ready)

        @block.tensor
        def _(pe):
            def tok(t):
                return slice(P * t, P * t + P)

            def products(dst, lh, ll, w_hi, w_lo, start, stop):
                pe.matmul(dst, lh, w_hi, start=start, stop=False)
                pe.matmul(dst, lh, w_lo, start=False, stop=False)
                return pe.matmul(dst, ll, w_hi, start=False, stop=stop)

            def square(u, k0, lh, ll, banks, start, stop, c=0):
                pe.wait_ge(low_done, u + 1 + 6 * c)
                for j in range(2):
                    w = slice(512 * j, 512 * j + 512)
                    for t in range(NT):
                        ins = products(bank[banks + t][:, :], lh[:, k0 + j, tok(t)], ll[:, k0 + j, tok(t)],
                                       wh[:, u % NSPLIT, w], wl[:, u % NSPLIT, w], start and j == 0, stop and j == 1)
                ins.then_inc(units_used, 1)

            def chunk(u, banks, fill, kts=KT, lh=aTh, ll=aTl, k0=0, between=None):
                n = kts // 2
                for i in range(n):
                    if between is not None and i == n // 2:
                        between()
                    if fill is not None:
                        pe.wait_ge(a_low, 8 * fill + 2 * i + 2)
                    square(u + i, k0 + 2 * i, lh, ll, banks, i == 0, i == n - 1)

            def xt_half(norm, fill, half):
                if norm == 0:
                    pe.wait_ge(x_loaded[half], 16)
                else:
                    pe.wait_ge(x_ready, 4 * (norm - 1) + 2 * half + 2)
                for g in (2 * half, 2 * half + 1):
                    if g >= 2:
                        pe.wait_ge(a_low, 8 * fill + 2 * g - 2)
                    for j in range(2):
                        for t in range(NT):
                            ins = pe.transpose(bank[6 + g % 2][:, T * j + P * t:T * j + P * t + P],
                                               x[:, t, tok(2 * g + j)], ident[:])
                    ins.then_inc(xt_psum, 1)

            def ffn(f):
                u, norm, fill = FIRST[f"ffn{f}"], FFN_NORM[f], FFN_FILL[f]
                acc = [[bank[2 + 2 * n + t] for n in range(2)] for t in range(NT)]

                def gate_up(c):
                    for i in range(4):
                        square(u + 4 + i, 2 * i, aTh, aTl, 0, i == 0, i == 3, c)

                def transpose_hidden(c):
                    for t in range(NT):
                        pe.wait_ge(h_ready, 2 * NFC * f + t + 1 + 2 * c)
                        for j in range(2):
                            ins = pe.transpose(bank[6][:, T * j + P * t:T * j + P * t + P], hid[:, t, tok(j)], ident[:])
                    ins.then_inc(ht_psum, 1)

                def down_part(u_slot, k, n, stop):
                    w = slice(512 * n, 512 * n + 512)
                    for t in range(NT):
                        ins = products(acc[t][n][:, :], hTh[:, k, tok(t)], hTl[:, k, tok(t)],
                                       wh[:, u_slot % NSPLIT, w], wl[:, u_slot % NSPLIT, w], False, stop)
                    return ins

                xt_half(norm, fill, 0)

                def second_half():
                    xt_half(norm, fill, 1)
                    for t in range(NT):
                        for n in range(2):
                            pe.matmul(acc[t][n][:, :], zeros[:, 0:P], zeros[:, :], start=True, stop=False)

                chunk(u, 0, fill, between=second_half)
                transpose_hidden(0)
                with pe.Fori(0, NFC - 1, 1) as c:
                    gate_up(c)
                    pe.wait_ge(ht_low, NFC * f + 1 + c)
                    for k in range(2):
                        pe.wait_ge(low_done, u + 9 + k + 6 * c)
                        for n in range(2):
                            ins = down_part(u + 8 + k, k, n, False)
                        ins.then_inc(units_used, 1)
                    transpose_hidden(c + 1)
                pe.wait_ge(ht_low, NFC * f + NFC)
                pe.wait_ge(low_done, u + 66)
                down_part(u + 64, 0, 0, False)
                down_part(u + 65, 1, 0, True).then_inc(acc_half, 1)
                for k in range(2):
                    down_part(u + 64 + k, k, 1, k == 1).then_inc(units_used, 1)

            pe.wait_ge(ident_in, 16)
            pe.wait_ge(rows_in, 16 * len(ROWS))
            pe.transpose(bank[0][:, 0:NCOL], vrows[:, :], ident[0:NCOL, 0:NCOL]).then_inc(vecs_psum, 1)
            pe.wait_ge(const_set, 3)
            pe.wait_ge(vecs_ready, 1)
            ffn(0)

            u0 = FIRST["w_in"]
            xt_half(1, 1, 0)

            def second_half():
                xt_half(1, 1, 1)
                pe.wait_ge(ws_in, 16)
                for g in range(4):
                    ins = pe.transpose(bank[4][:, tok(g)], ws_raw[:, g, :], ident[:])
                ins.then_inc(ws_psum, 1)

            chunk(u0, 0, 1, between=second_half)
            def qt(at, k, m, ready):
                ready()
                if k >= 1:
                    pe.wait_ge(at.qt_evac_a, k)
                    pe.wait_ge(at.qt_evac_d, k)
                for g in range(2):
                    for j in range(2):
                        for t in range(NT):
                            ins = pe.transpose(bank[6 + g][:, T * j + P * t:T * j + P * t + P],
                                               z[:, t, m, tok(2 * g + j)], ident[:])
                    ins.then_inc(at.qt_psum, 1)

            def evacuated(n):
                pe.wait_ge(mix_evac_a, n)
                pe.wait_ge(mix_evac_d, n)

            chunk(u0 + 4, 2, None)
            pe.wait_ge(ws_copied, 1)
            chunk(u0 + 8, 4, None)
            qt(mix_at, 0, 0, lambda: evacuated(1))
            chunk(u0 + 12, 0, None)
            qt(mix_at, 1, 1, lambda: evacuated(2))
            chunk(u0 + 16, 2, None)
            evacuated(3)
            chunk(u0 + 20, 4, None)
            qt(mix_at, 2, 3, lambda: pe.wait_ge(rope_done, 1))
            qt(mix_at, 3, 4, lambda: None)

            def scores(at, heads, i):
                kind, h = heads[i]
                if i >= 2:
                    pe.wait_ge(at.s_read, i - 1)
                b = bank[4 + i % 2]
                if kind == "fox":
                    q, k = augT[0:66, 0, h, :], augT[0:66, 1, h, :]
                else:
                    r = slice(64 * (h % 2), 64 * (h % 2) + 64)
                    m = 0 if kind == "sb" else 2
                    q, k = qkT[r, m, h // 2, :], qkT[r, m + 1, h // 2, :]
                pe.matmul(b[:, 0:P], q[:, 0:P], k[:, 0:P], start=True, stop=True)
                pe.matmul(b[:, P:3 * P], q[:, P:T], k[:, 0:T], start=True, stop=True).then_inc(at.s_psum, 1)

            def transpose_probs(at, heads, i):
                n_sb = sum(k == "sb" for k, _ in heads)
                if heads[i][0] == "sb":
                    pe.wait_ge(at.sb_probs, i + 1)
                else:
                    pe.wait_ge(at.sm_probs, i + 1 - n_sb)
                if i >= 1:
                    pe.wait_ge(at.pt_evac, i)
                for j in range(3):
                    ins = pe.transpose(bank[6][:, tok(j)], probs[:, i % 4, tok(j)], ident[:])
                ins.then_inc(at.pt_psum, 1)

            def outputs(at, heads, i, v):
                kind, h = heads[i]
                pe.wait_ge(at.pt_evac, i + 1)
                if i >= 2 and i % 2 == 0:
                    pe.wait_ge(at.y_low, i // 2)
                r = slice(64 * (h % 2), 64 * (h % 2) + 64)
                a = T * ((i // 2) % 2)
                pT = probsT[:, i % 2, :]
                pe.matmul(bank[7][r, a:a + T], v[:, 0, head_cols(h)], pT[:, 0:T], start=True, stop=False)
                pe.matmul(bank[7][r, a + P:a + T], v[:, 1, head_cols(h)], pT[:, T:T + P], start=False, stop=True)\
                    .then_inc(at.pv_psum, 1)

            def head_steps(at, heads, i, values):
                n = len(heads)
                if i < n:
                    scores(at, heads, i)
                if A_LAG <= i < n + A_LAG:
                    transpose_probs(at, heads, i - A_LAG)
                if A_LAG + 1 <= i < n + A_LAG + 1:
                    outputs(at, heads, i - A_LAG - 1, values(heads[i - A_LAG - 1][0]))

            evacuated(6)
            pe.wait_ge(mix_at.qt_evac_a, 4)
            pe.wait_ge(mix_at.qt_evac_d, 4)
            for i in range(20):
                if i < 16:
                    m = 6 + i // 4
                    if m >= 8 and i % 4 == 0:
                        pe.wait_ge(gate_evac, 2 * (m - 7))
                    square(u0 + 24 + i, 2 * (i % 4), aTh, aTl, W_IN_BANKS[m], i % 4 == 0, i % 4 == 3)
                else:
                    n, j = divmod(i - 16, 2)
                    if j == 0:
                        pe.wait_ge(gate_evac, 6 + 2 * n)
                        pe.wait_ge(mix_at.y_low, 4)
                    square(FIRST["branch_sb"] + i - 16, 2 * j, yTh, yTl, 2 * n, j == 0, j == 1)
                head_steps(mix_at, MIX_HEADS, i, lambda kind: z[:, :, 2 if kind == "sb" else 5, :])
            pe.wait_ge(mix_at.y_low, 8)
            for n in range(2):
                chunk(FIRST["branch_moba"] + 2 * n, 4 + 2 * n, None, 4, yTh, yTl, 4)

            def merged_half(half):
                pe.wait_ge(mg_ready, 2 * half + 2)
                for g in (2 * half, 2 * half + 1):
                    for j in range(2):
                        for t in range(NT):
                            ins = pe.transpose(bank[g][:, T * j + P * t:T * j + P * t + P], gates[:, t, tok(2 * g + j)], ident[:])
                    ins.then_inc(mgt_psum, 1)

            merged_half(0)
            for n in range(2):
                for i in range(4):
                    if n == 0 and i == 2:
                        merged_half(1)
                    if n == 0:
                        pe.wait_ge(mgt_low, i + 1)
                    square(FIRST["w_out"] + 4 * n + i, 2 * i, yTh, yTl, 4 - 2 * n, i == 0, i == 3)

            ffn(1)

            u0 = FIRST["e_in"]
            xt_half(3, 3, 0)
            chunk(u0, 0, 3, between=lambda: xt_half(3, 3, 1))
            pe.wait_ge(wf_low, 1)
            for t in range(NT):
                for k in range(KT):
                    ins = products(bank[4 + t][:, 0:8], aTh[:, k, tok(t)], aTl[:, k, tok(t)], wfh[:, k, :], wfl[:, k, :],
                                   k == 0, k == KT - 1)
            ins.then_inc(f_psum, 1)
            pe.wait_ge(mem_in, 16)
            for g in range(4):
                if g >= 2:
                    pe.wait_ge(mt_evac[g % 2], 1)
                for j in range(2):
                    for t in range(NT):
                        ins = pe.transpose(bank[6 + g % 2][:, T * j + P * t:T * j + P * t + P], mem_x[:, t, tok(2 * g + j)], ident[:])
                ins.then_inc(mt_psum, 1)
            chunk(u0 + 4, 2, None)
            pe.wait_ge(f_ready, 1)
            pe.matmul(bank[5][:, 0:8], tri[:], logf[:, 0, :], start=True, stop=True)
            pe.matmul(bank[5][:, 8:16], ones[:, 0:P], logf[:, 0, :], start=True, stop=False)
            pe.matmul(bank[5][:, 8:16], tri[:], logf[:, 1, :], start=False, stop=True).then_inc(cum_psum, 1)
            pe.wait_ge(aug_ready, 1)
            chunk(u0 + 8, 4, None)
            pe.wait_ge(even_evac_a, 1)
            pe.wait_ge(even_evac_d, 1)
            chunk(u0 + 12, 0, None)

            def aug_t(m):
                pe.wait_ge(heads_normed, m + 1)
                for g in range(4):
                    n = 2 * m + g // 2
                    if n >= 1:
                        if g % 2 == 0:
                            pe.wait_ge(fox_at.qt_evac_a, n)
                        else:
                            pe.wait_ge(fox_at.qt_evac_d, n)
                    for j in range(2):
                        for t in range(NT):
                            ins = pe.transpose(bank[6 + g % 2][0:66, T * j + P * t:T * j + P * t + P], aug[:, m, t, 2 * g + j, :], ident[:])
                    ins.then_inc(fox_at.qt_psum, 1)

            aug_t(0)
            pe.wait_ge(even_evac_a, 2)
            pe.wait_ge(even_evac_d, 2)
            chunk(u0 + 16, 2, None)
            aug_t(1)
            pe.wait_ge(vn_ready, 1)
            pe.wait_ge(ws_ready, 1)
            pe.wait_ge(even_evac_a, 3)
            for t in range(NT):
                for g in range(4):
                    ins = pe.matmul(bank[4 + t][:, tok(g)], wsT[:, g, :], z[:, t, 3, tok(g)], start=True, stop=True)
            ins.then_inc(sgu_psum, 1)
            pe.wait_ge(even_evac_a, 4)

            def mem_unit(u, banks, i, fill):
                if fill is not None:
                    pe.wait_ge(a_low, 8 * fill + 2 * i + 2)
                square(u + i, 2 * i, aTh, aTl, banks, i == 0, i == 3)

            mem_unit(FIRST["mem_k0"], 0, 0, 4)
            pe.wait_ge(ya_ready, 2)
            pe.wait_ge(fox_at.qt_evac_a, 4)
            pe.wait_ge(fox_at.qt_evac_d, 4)
            for g in range(2):
                for j in range(2):
                    for t in range(NT):
                        ins = pe.transpose(bank[6 + g][:, T * j + P * t:T * j + P * t + P], z[:, t, 2, tok(2 * g + j)], ident[:])
                ins.then_inc(ya_psum, 1)
            pe.wait_ge(even_evac_a, 5)
            pe.wait_ge(even_evac_d, 3)

            def out_unit(name, i):
                n, g = MIX_OUT[i]
                square(FIRST[name] + i, 2 * g, yTh, yTl, 2 * n, g == 0, g == 3)

            for i in range(12):
                if i < 3:
                    mem_unit(FIRST["mem_k0"], 0, i + 1, 4)
                elif i < 7:
                    mem_unit(FIRST["mem_v0"], 2, i - 3, None)
                elif i < 11:
                    if i == 7:
                        pe.wait_ge(ya_low, 2)
                        pe.wait_ge(memk_evac_a, 1)
                        pe.wait_ge(memk_evac_d, 1)
                    if i == 9:
                        pe.wait_ge(memv_evac_a, 1)
                        pe.wait_ge(memv_evac_d, 1)
                    out_unit("e_out", i - 7)
                if i == 3:
                    pe.wait_ge(ya_low, 2)
                head_steps(fox_at, FOX_HEADS, i, lambda kind: z[:, :, 4, :])
            pe.wait_ge(fox_at.y_low, 4)
            for i in range(4, 8):
                out_unit("e_out", i)

            def cross(l, fill, n_normed):
                at, norm, u = xa_at[l], 4 + 3 * l, FIRST[f"xq{l}"]
                xt_half(norm, fill, 0)
                chunk(u, 0, fill, between=lambda: xt_half(norm, fill, 1))

                def heads_t(src, n):
                    if n > 0:
                        pe.wait_ge(at.qt_evac_a, n)
                        pe.wait_ge(at.qt_evac_d, n)
                    for g in range(2):
                        for j in range(2):
                            for t in range(NT):
                                ins = pe.transpose(bank[6 + g][:, T * j + P * t:T * j + P * t + P], src[:, t, tok(2 * g + j)], ident[:])
                        ins.then_inc(at.qt_psum, 1)

                pe.wait_ge(heads_normed, n_normed)
                heads_t(kz, 0)
                if l == 0:
                    for i in range(4):
                        mem_unit(FIRST["mem_k1"], 2, i, 6)
                pe.wait_ge(heads_normed, n_normed + 1)
                heads_t(z[:, :, 0, :], 1)
                pe.wait_ge(at.qt_evac_a, 2)
                pe.wait_ge(at.qt_evac_d, 2)
                pe.wait_ge(memv_evac_a, l + 1)
                pe.wait_ge(memv_evac_d, l + 1)
                if l == 0:
                    pe.wait_ge(even_evac_a, 6)
                    pe.wait_ge(even_evac_d, 4)
                for i in range(7):
                    if l == 0 and i < 4:
                        mem_unit(FIRST["mem_v1"], 0, i, None)
                    if i < 4:
                        if i >= 2:
                            pe.wait_ge(at.sm_exp, i - 1)
                        for t in range(NT):
                            ins = pe.matmul(bank[4 + i % 2][:, T * t:T * t + T], qTx[:, i, tok(t)], kTm[:, i, :], start=True, stop=True)
                        ins.then_inc(at.s_psum, 1)
                    if 2 <= i < 6:
                        j = i - 2
                        pe.wait_ge(at.sm_probs, j + 1)
                        if j >= 1:
                            pe.wait_ge(at.pt_evac, j)
                        for k in range(2):
                            for t in range(NT):
                                ins = pe.transpose(bank[6][:, T * k + P * t:T * k + P * t + P],
                                                   probs[:, j, T * t + P * k:T * t + P * k + P], ident[:])
                        ins.then_inc(at.pt_psum, 1)
                    if 3 <= i:
                        j = i - 3
                        pe.wait_ge(at.pt_evac, j + 1)
                        if j >= 1:
                            pe.wait_ge(at.y_low, j)
                        for k in range(2):
                            ins = pe.matmul(bank[7][:, 0:T], vm[l][:, k, tok(j)], probsT[:, j % 2, T * k:T * k + T],
                                            start=k == 0, stop=k == 1)
                        ins.then_inc(at.pv_psum, 1)
                pe.wait_ge(at.y_low, 4)
                for n in range(2):
                    if l == 0 and n == 0:
                        pe.wait_ge(memv_evac_a, 2)
                        pe.wait_ge(memv_evac_d, 2)
                        pe.wait_ge(memk_evac_a, 2)
                        pe.wait_ge(memk_evac_d, 2)
                    chunk(FIRST[f"xo{l}"] + 2 * n, 2 * n, None, 4, yTh, yTl)

            cross(0, 5, 3)
            ffn(2)

            u0 = FIRST["o_in"]

            def odd_evacuated(n):
                pe.wait_ge(odd_evac_a, n)
                pe.wait_ge(odd_evac_d, n)

            xt_half(6, 8, 0)
            chunk(u0, 0, 8, between=lambda: xt_half(6, 8, 1))
            chunk(u0 + 4, 2, None)
            odd_evacuated(1)
            pe.wait_ge(band_in, 32)
            for g in range(4):
                b, a = bank[4 + g // 2], T * (g % 2)
                pe.matmul(b[:, a:a + T], z[:, 0, 0, tok(g)], band[:, g, 0:T], start=True, stop=False)
                ins = pe.matmul(b[:, a + P:a + T], z[:, 1, 0, tok(g)], band[:, g, T:], start=False, stop=True)
                if g % 2:
                    ins.then_inc(pool_psum, 1)
            chunk(u0 + 8, 0, None)
            pe.wait_ge(pool_evac[0], 1)
            pe.wait_ge(pool_evac[1], 1)
            for g in range(4):
                ins = pe.matmul(bank[6 + g // 2][:, T * (g % 2):T * (g % 2) + T], wpool[:, g, :], poolT[:, g, :], start=True, stop=True)
                if g % 2:
                    ins.then_inc(yc_psum, 1)
            odd_evacuated(2)
            chunk(u0 + 12, 2, None)

            def blocks_t(src, first, done):
                for g in range(2):
                    for j in range(2):
                        for t in range(NT):
                            ins = pe.transpose(bank[first + g][:, T * j + P * t:T * j + P * t + P], src[:, t, tok(2 * g + j)], ident[:])
                    ins.then_inc(done, 1)

            pe.wait_ge(xg_ready, 1)
            blocks_t(z[:, :, 1, :], 4, xgt_psum)
            odd_evacuated(4)
            pe.wait_ge(yc_low, 4)
            blocks_t(z[:, :, 3, :], 6, gbt_psum)
            for i in range(8):
                if i == 4:
                    pe.wait_ge(yd_low, 2)
                out_unit("o_out", i)

            cross(1, 9, 5)
            ffn(3)


RSTD_ORDER = {0: 0, 1: 1, 2: 2, 11: 3, 3: 4, 9: 5, 4: 6, 5: 7, 6: 8, 7: 9, 8: 10}

INPUTS = ["x", "positions", "ffn1_norm", "ffn1_w_gate", "ffn1_w_up", "ffn1_w_down", "mix_norm", "w_in", "b_gate",
          "w_branch_moba", "w_branch_sb", "w_out", "ffn2_norm", "ffn2_w_gate", "ffn2_w_up", "ffn2_w_down",
          "final_norm", "mem_2", "g_mix_2", "g_xa_2", "g_mem_2", "xa_wq_2", "xa_wkv_2", "xa_wo_2", "xa_gq_2",
          "xa_gk_2", "g_ffn_2", "w_gate_2", "w_up_2", "w_down_2", "e_w_in_2", "e_b_f_2", "e_g_v_2", "e_w_s_2",
          "e_b_s_2", "e_g_qn_2", "e_g_kn_2", "e_w_out_2", "o_w_in_2", "o_w_pool_2", "o_s_pool_2", "o_conv_w_2",
          "o_w_out_2"]


def kernel(**inputs):
    import concourse.bacc as bacc
    from concourse.bass_utils import run_bass_kernel_spmd

    nc = bacc.Bacc("TRN2", target_bir_lowering=False, num_devices=1)
    arrays, aps = {}, {}
    for name in INPUTS:
        arrays[name] = np.ascontiguousarray(inputs[name])
    arrays.update(shape_constants())
    for name, a in arrays.items():
        aps[name] = nc.dram_tensor(name, a.shape, mybir.dt.from_np(a.dtype), kind="ExternalInput").ap()
    out = nc.dram_tensor("out", (1, T, D), F32, kind="ExternalOutput").ap()
    two_block_kernel(nc, aps, out)
    result = run_bass_kernel_spmd(nc, [arrays], core_ids=[0])
    return result.results[0]["out"]
```
